# Optimizing a Trainium2 kernel written in Bass

```python
import math
import jax, jax.numpy as jnp
from jax import lax
import numpy as np

D_MODEL = 1024
BATCH = 1
SEQ = 2048
DEPTH = 1
DEC_BATCH = 8
DEC_SEQ = 4
PAST_LEN = 2048
PAGE_SIZE = 128

HEAD_DIM = 64
ATT_WIDTH = D_MODEL // 2
ATT_HEADS = ATT_WIDTH // HEAD_DIM
SSM_WIDTH = D_MODEL - ATT_WIDTH
SSM_CH = 16
SSM_GROUPS = SSM_WIDTH // SSM_CH
SSM_STATE = 64
DILATIONS = ((128, 1), (512, 4), (2048, 16))
MAX_SPAN = max(w for w, _ in DILATIONS)
Q_BLOCK = 128
FFN_HIDDEN = -(-8 * D_MODEL // (3 * 256)) * 256
N_MOD = 6
EPS = 1e-6

kernel_name = 'hymba_s5_longnet_decode_step'

def rms_norm(x, gain):
    xf = x.astype(jnp.float32)
    return xf * lax.rsqrt(jnp.mean(xf * xf, axis=-1, keepdims=True) + EPS) * gain.astype(jnp.float32)

def ada_modulation(c, w_ada, b_ada):
    mod = jax.nn.silu(c.astype(jnp.float32)) @ w_ada.astype(jnp.float32) + b_ada.astype(jnp.float32)
    return jnp.split(mod[:, None, :], N_MOD, axis=-1)

def combine_dilations(outs, lses):
    w = jax.nn.softmax(jnp.stack(lses, axis=0), axis=0)
    return jnp.einsum('pbth,pbthd->bthd', w, jnp.stack(outs, axis=0))

def dilated_band_attention(q, k, v, dil, n_back):
    b, s, h, dh = q.shape
    n = s // dil
    n_pad = -(-n // Q_BLOCK) * Q_BLOCK
    nb = n_pad // Q_BLOCK
    z = b * dil

    def to_sub(a):
        a = a.reshape(b, n, dil, h, dh).transpose(0, 2, 1, 3, 4).reshape(z, n, h, dh)
        return jnp.pad(a, ((0, 0), (0, n_pad - n), (0, 0), (0, 0)))

    qs, ks, vs = to_sub(q), to_sub(k), to_sub(v)
    front = ((0, 0), (Q_BLOCK, 0), (0, 0), (0, 0))

    def blocks_with_prev(a):
        a = jnp.pad(a, front)
        prev = a[:, :n_pad].reshape(z, nb, Q_BLOCK, h, dh)
        cur = a[:, Q_BLOCK:].reshape(z, nb, Q_BLOCK, h, dh)
        return jnp.concatenate([prev, cur], axis=2)

    kb, vb = blocks_with_prev(ks), blocks_with_prev(vs)
    qb = qs.reshape(z, nb, Q_BLOCK, h, dh)
    scores = jnp.einsum('znqhd,znkhd->znhqk', qb, kb) * (HEAD_DIM ** -0.5)
    qi = jnp.arange(Q_BLOCK)[:, None]
    ki = jnp.arange(2 * Q_BLOCK)[None, :]
    dist = qi + Q_BLOCK - ki
    blk = jnp.arange(nb)[:, None, None]
    valid = (dist >= 0) & (dist <= n_back) & (blk * Q_BLOCK - Q_BLOCK + ki >= 0)
    scores = jnp.where(valid[None, :, None], scores, -jnp.inf)
    lse = jax.nn.logsumexp(scores, axis=-1)
    p = jnp.exp(scores - lse[..., None])
    o = jnp.einsum('znhqk,znkhd->znqhd', p, vb).reshape(z, n_pad, h, dh)[:, :n]
    lse = lse.transpose(0, 1, 3, 2).reshape(z, n_pad, h)[:, :n]
    o = o.reshape(b, dil, n, h, dh).transpose(0, 2, 1, 3, 4).reshape(b, s, h, dh)
    lse = lse.reshape(b, dil, n, h).transpose(0, 2, 1, 3).reshape(b, s, h)
    return o, lse

def dilated_gather_attention(q, k_all, v_all, n_past):
    t = q.shape[1]
    outs, lses = [], []
    for window, dil in DILATIONS:
        n_back = window // dil
        idx = n_past + jnp.arange(t)[:, None] - dil * jnp.arange(n_back + 1)[None, :]
        valid = idx >= 0
        idx = jnp.maximum(idx, 0)
        kg, vg = k_all[:, idx], v_all[:, idx]
        scores = jnp.einsum('bthd,btmhd->bthm', q, kg) * (HEAD_DIM ** -0.5)
        scores = jnp.where(valid[None, :, None, :], scores, -jnp.inf)
        lse = jax.nn.logsumexp(scores, axis=-1)
        p = jnp.exp(scores - lse[..., None])
        outs.append(jnp.einsum('bthm,btmhd->bthd', p, vg))
        lses.append(lse)
    return combine_dilations(outs, lses)

def attend_prompt(q, k, v):
    outs, lses = [], []
    for window, dil in DILATIONS:
        o, l = dilated_band_attention(q, k, v, dil, window // dil)
        outs.append(o)
        lses.append(l)
    keep = min(MAX_SPAN, q.shape[1])
    return combine_dilations(outs, lses), k[:, -keep:], v[:, -keep:]

def make_sample_attend(cache_k, cache_v):
    def attend(q, k, v):
        n_past, t = cache_k.shape[1], q.shape[1]
        k_all = jnp.concatenate([cache_k.astype(jnp.float32), k], axis=1)
        v_all = jnp.concatenate([cache_v.astype(jnp.float32), v], axis=1)
        o = dilated_gather_attention(q, k_all, v_all, n_past)
        return o, k_all[:, t:], v_all[:, t:]
    return attend

def _linear_combine(left, right):
    a_l, b_l = left
    a_r, b_r = right
    return a_r * a_l, a_r * b_l + b_r

def s5_mixer(u, h0, a_re, a_im, log_dt, b_re, b_im, c_re, c_im, d_skip, w_glu):
    f32 = jnp.float32
    bsz, t, _ = u.shape
    u = u.astype(f32)
    a = lax.complex(a_re.astype(f32), a_im.astype(f32))
    dt = jnp.exp(log_dt.astype(f32))[:, None]
    a_bar = jnp.exp(dt * a)
    b_bar = ((a_bar - 1.0) / a)[..., None] * lax.complex(b_re.astype(f32), b_im.astype(f32))
    c_mat = lax.complex(c_re.astype(f32), c_im.astype(f32))
    ug = u.reshape(bsz, t, SSM_GROUPS, SSM_CH).astype(jnp.complex64)
    bu = jnp.einsum('btgc,gnc->btgn', ug, b_bar)
    if h0 is not None:
        bu = bu.at[:, 0].add(a_bar * h0)
    a_seq = jnp.broadcast_to(a_bar, bu.shape)
    _, h = lax.associative_scan(_linear_combine, (a_seq, bu), axis=1)
    y = jnp.einsum('gcn,btgn->btgc', c_mat, h).real.reshape(bsz, t, SSM_WIDTH) + d_skip.astype(f32) * u
    y = jax.nn.gelu(y)
    y = y * jax.nn.sigmoid(y @ w_glu.astype(f32))
    return y, h[:, -1]

def decoder_layer(x, c, attend, h0, norm1_g, norm2_g, w_ada, b_ada, w_in, q_gain, k_gain,
                  ssm_a_re, ssm_a_im, ssm_log_dt, ssm_b_re, ssm_b_im, ssm_c_re, ssm_c_im, ssm_d, w_glu,
                  attn_out_g, ssm_out_g, w_out, w_gate, w_up, w_down):
    f32 = jnp.float32
    bsz, t, _ = x.shape
    shift1, scale1, gate1, shift2, scale2, gate2 = ada_modulation(c, w_ada, b_ada)
    h = rms_norm(x, norm1_g) * (1.0 + scale1) + shift1
    zcols = h @ w_in.astype(f32)
    q = zcols[..., :ATT_WIDTH].reshape(bsz, t, ATT_HEADS, HEAD_DIM)
    k = zcols[..., ATT_WIDTH:2 * ATT_WIDTH].reshape(bsz, t, ATT_HEADS, HEAD_DIM)
    v = zcols[..., 2 * ATT_WIDTH:3 * ATT_WIDTH].reshape(bsz, t, ATT_HEADS, HEAD_DIM)
    u = zcols[..., 3 * ATT_WIDTH:]
    q = rms_norm(q, q_gain)
    k = rms_norm(k, k_gain)
    o_att, k_keep, v_keep = attend(q, k, v)
    y_ssm, h_last = s5_mixer(u, h0, ssm_a_re, ssm_a_im, ssm_log_dt, ssm_b_re, ssm_b_im,
                             ssm_c_re, ssm_c_im, ssm_d, w_glu)
    merged = jnp.concatenate([rms_norm(o_att.reshape(bsz, t, ATT_WIDTH), attn_out_g),
                              rms_norm(y_ssm, ssm_out_g)], axis=-1)
    x1 = x.astype(f32) + gate1 * (merged @ w_out.astype(f32))
    h2 = rms_norm(x1, norm2_g) * (1.0 + scale2) + shift2
    ff = (jax.nn.silu(h2 @ w_gate.astype(f32)) * (h2 @ w_up.astype(f32))) @ w_down.astype(f32)
    y = x1 + gate2 * ff
    return y.astype(x.dtype), k_keep, v_keep, h_last

def setup_inputs(seed: int = 0) -> dict:
    key = jax.random.key(seed)
    ks = jax.random.split(key, 32)
    f32 = jnp.float32
    L = DEPTH
    n_buf = min(MAX_SPAN, PAST_LEN)

    def nrm(k, shape, scale):
        return jax.random.normal(k, shape, f32) * scale

    n_idx = jnp.arange(SSM_STATE, dtype=f32)
    return {
        'x_prompt': nrm(ks[0], (BATCH, SEQ, D_MODEL), 1.0),
        'x_sample': nrm(ks[1], (DEC_BATCH, DEC_SEQ, D_MODEL), 1.0),
        'cache_k': nrm(ks[2], (L, DEC_BATCH, n_buf, ATT_HEADS, HEAD_DIM), 1.0),
        'cache_v': nrm(ks[3], (L, DEC_BATCH, n_buf, ATT_HEADS, HEAD_DIM), 1.0),
        'state_ssm_re': nrm(ks[4], (L, DEC_BATCH, SSM_GROUPS, SSM_STATE), 0.3),
        'state_ssm_im': nrm(ks[5], (L, DEC_BATCH, SSM_GROUPS, SSM_STATE), 0.3),
        'c_prompt': nrm(ks[6], (BATCH, D_MODEL), 1.0),
        'c_sample': nrm(ks[7], (DEC_BATCH, D_MODEL), 1.0),
        'norm1_g': 1.0 + nrm(ks[8], (L, D_MODEL), 0.02),
        'norm2_g': 1.0 + nrm(ks[9], (L, D_MODEL), 0.02),
        'w_ada': nrm(ks[10], (L, D_MODEL, N_MOD * D_MODEL), 0.5 * D_MODEL ** -0.5),
        'b_ada': nrm(ks[11], (L, N_MOD * D_MODEL), 0.02),
        'w_in': nrm(ks[12], (L, D_MODEL, 3 * ATT_WIDTH + SSM_WIDTH), D_MODEL ** -0.5),
        'q_gain': 1.0 + nrm(ks[13], (L, HEAD_DIM), 0.02),
        'k_gain': 1.0 + nrm(ks[14], (L, HEAD_DIM), 0.02),
        'ssm_a_re': -0.5 + nrm(ks[15], (L, SSM_GROUPS, SSM_STATE), 0.01),
        'ssm_a_im': math.pi * n_idx + nrm(ks[16], (L, SSM_GROUPS, SSM_STATE), 0.01),
        'ssm_log_dt': jax.random.uniform(ks[17], (L, SSM_GROUPS), f32, math.log(1e-3), math.log(1e-1)),
        'ssm_b_re': nrm(ks[18], (L, SSM_GROUPS, SSM_STATE, SSM_CH), (2 * SSM_CH) ** -0.5),
        'ssm_b_im': nrm(ks[19], (L, SSM_GROUPS, SSM_STATE, SSM_CH), (2 * SSM_CH) ** -0.5),
        'ssm_c_re': nrm(ks[20], (L, SSM_GROUPS, SSM_CH, SSM_STATE), (2 * SSM_STATE) ** -0.5),
        'ssm_c_im': nrm(ks[21], (L, SSM_GROUPS, SSM_CH, SSM_STATE), (2 * SSM_STATE) ** -0.5),
        'ssm_d': nrm(ks[22], (L, SSM_WIDTH), 1.0),
        'w_glu': nrm(ks[23], (L, SSM_WIDTH, SSM_WIDTH), SSM_WIDTH ** -0.5),
        'attn_out_g': 1.0 + nrm(ks[24], (L, ATT_WIDTH), 0.02),
        'ssm_out_g': 1.0 + nrm(ks[25], (L, SSM_WIDTH), 0.02),
        'w_out': nrm(ks[26], (L, D_MODEL, D_MODEL), D_MODEL ** -0.5),
        'w_gate': nrm(ks[27], (L, D_MODEL, FFN_HIDDEN), D_MODEL ** -0.5),
        'w_up': nrm(ks[28], (L, D_MODEL, FFN_HIDDEN), D_MODEL ** -0.5),
        'w_down': nrm(ks[29], (L, FFN_HIDDEN, D_MODEL), FFN_HIDDEN ** -0.5),
    }

def reference(x_prompt, x_sample, cache_k, cache_v, state_ssm_re, state_ssm_im, c_prompt, c_sample,
              norm1_g, norm2_g, w_ada, b_ada, w_in, q_gain, k_gain,
              ssm_a_re, ssm_a_im, ssm_log_dt, ssm_b_re, ssm_b_im, ssm_c_re, ssm_c_im, ssm_d, w_glu,
              attn_out_g, ssm_out_g, w_out, w_gate, w_up, w_down):
    f32 = jnp.float32
    xp, xs = x_prompt, x_sample
    kp_l, vp_l, hp_l, ks_l, vs_l, hs_l = [], [], [], [], [], []
    for layer in range(DEPTH):
        w = tuple(p[layer] for p in (norm1_g, norm2_g, w_ada, b_ada, w_in, q_gain, k_gain,
                                     ssm_a_re, ssm_a_im, ssm_log_dt, ssm_b_re, ssm_b_im, ssm_c_re, ssm_c_im,
                                     ssm_d, w_glu, attn_out_g, ssm_out_g, w_out, w_gate, w_up, w_down))
        xp, kp, vp, hp = decoder_layer(xp, c_prompt, attend_prompt, None, *w)
        h0 = lax.complex(state_ssm_re[layer].astype(f32), state_ssm_im[layer].astype(f32))
        xs, ks_, vs_, hs = decoder_layer(xs, c_sample, make_sample_attend(cache_k[layer], cache_v[layer]), h0, *w)
        kp_l.append(kp); vp_l.append(vp); hp_l.append(hp)
        ks_l.append(ks_); vs_l.append(vs_); hs_l.append(hs)
    hp_all = jnp.stack(hp_l, axis=0)
    hs_all = jnp.stack(hs_l, axis=0)
    return (xp, xs, jnp.stack(kp_l, axis=0), jnp.stack(vp_l, axis=0), hp_all.real, hp_all.imag,
            jnp.stack(ks_l, axis=0), jnp.stack(vs_l, axis=0), hs_all.real, hs_all.imag)


_drawn_inputs = setup_inputs


def setup_inputs(seed=0):
    import zlib

    import numpy as np

    out = dict(_drawn_inputs(seed))
    spreads = {}
    factors = {'norm1_g': 3.086,
     'norm2_g': 8.0,
     'q_gain': 8.0,
     'k_gain': 2.928,
     'ssm_a_re': 3.662,
     'attn_out_g': 8.0,
     'ssm_out_g': 8.0}
    for name, (base, spread) in spreads.items():
        noise = np.random.default_rng([zlib.crc32(name.encode()), seed]).standard_normal(out[name].shape)
        drawn = base * np.exp(spread * noise) if base else spread * noise
        out[name] = __import__('jax').numpy.asarray(drawn.astype(out[name].dtype))
    for name, factor in factors.items():
        out[name] = (out[name] * factor).astype(out[name].dtype)
    return out
```

```python
import concourse.bass as bass
from concourse import mybir
from contextlib import ExitStack
import math

F32 = mybir.dt.float32
F32R = mybir.dt.float32r
ALU = mybir.AluOpType
ACT = mybir.ActivationFunctionType
AX = mybir.AxisListType

D = 1024
SEQ = 2048
NB, TS = 8, 4
NS = NB * TS
ROWS = SEQ + NS
HEADS, HD = 8, 64
AW = HEADS * HD
SW = D - AW
GROUPS, CH, ST = 32, 16, 64
PAST = 2048
FF = 2816
NMOD = 6
EPS = 1e-6
KT = D // 128


class Steps:

    def __init__(self, eng, sem, base=0):
        self.eng, self.sem, self.base, self.n = eng, sem, base, 0

    def did(self, instruction):
        instruction.then_inc(self.sem, 1)
        self.n += 1

    def wait(self):
        self.eng.wait_ge(self.sem, self.base + self.n)

    def link(self, instruction):
        self.did(instruction)
        self.wait()


class Pool_:

    def __init__(self, nc, ctx, suffix=""):
        self.nc, self.ctx, self.suffix, self.nums = nc, ctx, suffix, []
        ctx.callback(self.clear)

    def sb(self, name, shape, dt=F32):
        return self.ctx.enter_context(self.nc.sbuf_tensor(name + self.suffix, shape, dt))

    def ps(self, name, shape):
        return self.ctx.enter_context(self.nc.psum_tensor(name + self.suffix, shape, F32))

    def sem(self, name):
        handle = self.ctx.enter_context(self.nc.semaphore(name + self.suffix))
        self.nums.append(handle.num)
        return handle

    def clear(self):
        runs = []
        for x in sorted(self.nums):
            if runs and runs[-1][1] == x:
                runs[-1][1] = x + 1
            else:
                runs.append([x, x + 1])
        if runs:
            with self.nc.Block() as block:
                @block.gpsimd
                def _(pool):
                    for a, b in runs:
                        pool.sem_clear(range(a, b))

    def sem2(self, name):
        return [self.sem(f"{name}{p}") for p in range(2)]


class Turn:

    def __init__(self, add, i=None, mult=0):
        self.add, self.i, self.mult = add, i, mult

    def __add__(self, k):
        return Turn(self.add + k, self.i, self.mult)

    def times(self, num, den=1):
        c = self.add // den * num
        return c if self.i is None else self.i * (self.mult // den * num) + c

    @property
    def idx(self):
        return self.times(1)

    def slot(self, n):
        return self.add % n


def run_steps(eng, step, sections, mult):
    for first, end, looped in sections:
        if looped:
            with eng.Fori(0, (end - first) // mult) as i:
                for j in range(mult):
                    step(Turn(first + j, i, mult))
        else:
            for n in range(first, end):
                step(Turn(n))


def lookahead(eng, ahead, behind, tiles, sections):
    ahead(Turn(0))

    def step(n):
        if n.i is not None or n.add + 1 < tiles:
            ahead(n + 1)
        behind(n)

    run_steps(eng, step, sections, 2)


def wait(eng, sem, value):
    if not isinstance(value, int) or value > 0:
        eng.wait_ge(sem, value)


def is_sample(n):
    return n.i is None and n.add == SEQ // 128


def rows_of(n):
    return NS if is_sample(n) else 128


def tile_rows(n):
    if n.i is None:
        return slice(n.add * 128, n.add * 128 + rows_of(n))
    return bass.ds(n.times(128), 128)


def modulation_stage(nc, t, const, w_in_sb, s_win):
    NC = 1 + NB
    CW = 512
    CHUNKS = NMOD * D // CW
    TURNS = CHUNKS // 2
    with ExitStack() as ctx:
        P = Pool_(nc, ctx)
        c_sb = P.sb("c_sb", [NC, D])
        c_act = P.sb("c_act", [NC, D])
        cT = P.sb("cT", [128, KT, NC])
        w_ada = P.sb("w_ada_sb", [128, 2, KT, CW])
        b_ada = P.sb("b_ada_sb", [NC, 2, CW])
        mod = P.sb("mod_sb", [NC, 2, CW])
        cT_ps = P.ps("cT_ps", [128, 512])
        mod_ps = [P.ps(f"mod_ps{p}", [128, CW]) for p in range(2)]
        s_c, s_silu, s_cTp, s_cT = (P.sem(x) for x in ("m_c", "m_silu", "m_cTp", "m_cT"))
        s_w, s_mm, s_add, s_st = (P.sem2(x) for x in ("m_w", "m_mm", "m_add", "m_st"))
        block = ctx.enter_context(nc.Block())
        w_v = t["w_ada"].rearrange("(k p) n -> p k n", p=128)
        b_v = t["b_ada"].rearrange("(o n) -> o n", o=1)

        @block.sync
        def _(sp):
            sp.dma_start(c_sb[0:1, :], t["c_prompt"]).then_inc(s_c, 16)
            sp.dma_start(c_sb[1:NC, :], t["c_sample"]).then_inc(s_c, 16)
            with sp.Fori(0, TURNS) as i:
                for p in range(2):
                    sp.wait_ge(s_mm[p], i)
                    sp.wait_ge(s_add[p], i)
                    n = (i * 2 + p) * CW
                    sp.dma_start(w_ada[:, p], w_v[:, :, bass.ds(n, CW)]).then_inc(s_w[p], 16)
                    sp.dma_start(b_ada[:, p], b_v[:, bass.ds(n, CW)].broadcast_to([NC, CW])).then_inc(s_w[p], 16)
            w_in = t["w_in"].rearrange("(k p) n -> p k n", p=128)
            for c in range(2):
                sp.dma_start(w_in_sb[:, :, c * D:(c + 1) * D], w_in[:, :, c * D:(c + 1) * D]).then_inc(s_win, 16)

        @block.scalar
        def _(act):
            act.wait_ge(s_c, 32)
            act.activation(c_act[:, :], c_sb[:, :], ACT.Silu).then_inc(s_silu, 1)
            with act.Fori(0, TURNS) as i:
                for p in range(2):
                    act.wait_ge(s_add[p], i + 1)
                    act.dma_start(t["mod"][:, bass.ds((i * 2 + p) * CW, CW)], mod[:, p]).then_inc(s_st[p], 16)
            for p in range(2):
                act.wait_ge(s_st[p], 16 * TURNS)

        @block.tensor
        def _(pe):
            pe.wait_ge(s_silu, 1)
            for k in range(KT):
                mm = pe.transpose(cT_ps[:, k * NC:(k + 1) * NC], c_act[:, k * 128:(k + 1) * 128], const["ident"][0:NC, 0:NC])
            mm.then_inc(s_cTp, 1)
            pe.wait_ge(s_cT, 1)
            with pe.Fori(0, TURNS) as i:
                for p in range(2):
                    pe.wait_ge(s_w[p], i * 32 + 32)
                    pe.wait_ge(s_add[p], i)
                    for k in range(KT):
                        mm = pe.matmul(mod_ps[p][0:NC, :], cT[:, k, :], w_ada[:, p, k, :], start=(k == 0), stop=(k == KT - 1))
                    mm.then_inc(s_mm[p], 1)

        @block.vector
        def _(dve):
            dve.wait_ge(s_cTp, 1)
            dve.tensor_copy(cT[:, :, :], cT_ps[:, 0:KT * NC].rearrange("p (k n) -> p k n", n=NC)).then_inc(s_cT, 1)
            with dve.Fori(0, TURNS) as i:
                for p in range(2):
                    dve.wait_ge(s_mm[p], i + 1)
                    dve.wait_ge(s_st[p], i * 16)
                    dve.tensor_tensor(mod[:, p], mod_ps[p][0:NC, :], b_ada[:, p], ALU.add).then_inc(s_add[p], 1)


def load_modulation(sp, t, dst, which, sem, sample):
    if not sample:
        sp.dma_start(dst, t["mod"][0:1, which * D:(which + 1) * D].broadcast_to([128, D])).then_inc(sem, 16)
    else:
        m = t["mod"]
        src = bass.AP(m.tensor, (NMOD * D) + which * D, [[NMOD * D, NB], [0, TS], [1, D]])
        sp.dma_start(dst, src).then_inc(sem, 16)


def projection_stage(nc, t, const, w_in_sb, s_win):
    TILES = SEQ // 128 + 1
    SECTIONS = ((0, TILES - 3, True), (TILES - 3, TILES, False))
    with ExitStack() as ctx:
        P = Pool_(nc, ctx)
        A = P.sb("p_scale", [128, 2, D])
        B = P.sb("p_shift", [128, 2, D])
        g1 = P.sb("p_norm_g", [128, D])
        gqk = P.sb("p_gain_qk", [128, 2 * HD])
        x = P.sb("p_x", [128, 2, D])
        h = P.sb("p_h", [128, 2, D])
        hT = P.sb("p_hT", [128, 2, KT, 128])
        junk = P.sb("p_junk", [128, D])
        sq = P.sb("p_sq", [128, 2 * AW])
        qk = P.sb("p_qk", [128, 2, 2 * AW])
        vu = P.sb("p_vu", [128, 2, D])
        ss = P.sb("p_ss", [128, 2, 3])
        hss = P.sb("p_hss", [128, 2, 3, 2 * HEADS])
        hT_ps = P.ps("p_hT_ps", [128, D])
        out_ps = P.ps("p_out_ps", [128, 2 * D])
        s_g, s_A = P.sem("p_g"), P.sem("p_A")
        names = ("x", "root", "h", "hTp", "hTa", "hTd", "qkm", "vm", "um", "hsq", "hss", "hroot",
                 "qkn", "qkg", "ve", "ue", "qks", "vus")
        S = {n: P.sem2("p_" + n) for n in names}
        s_act, s_dve = P.sem("p_act"), P.sem("p_dve")
        block = ctx.enter_context(nc.Block())

        @block.sync
        def _(sp):
            sp.dma_start(x[:, 0], t["x_prompt"][0:128, :]).then_inc(S["x"][0], 16)
            sp.dma_start(x[:, 1], t["x_prompt"][128:256, :]).then_inc(S["x"][1], 16)
            sp.dma_start(g1[:, :], t["norm1_g"].rearrange("(o n) -> o n", o=1).broadcast_to([128, D])).then_inc(s_g, 16)
            load_modulation(sp, t, A[:, 0], 1, s_g, False)
            load_modulation(sp, t, B[:, 0], 0, s_g, False)
            load_modulation(sp, t, A[0:NS, 1], 1, s_g, True)
            load_modulation(sp, t, B[0:NS, 1], 0, s_g, True)
            for j, name in enumerate(("q_gain", "k_gain")):
                sp.dma_start(gqk[:, j * HD:(j + 1) * HD],
                             t[name].rearrange("(o n) -> o n", o=1).broadcast_to([128, HD])).then_inc(s_g, 16)

            def step(n):
                r, p, i = rows_of(n), n.slot(2), n.times(1, 2)
                if n.i is not None or n.add + 2 < TILES:
                    load = n + 2
                    sp.wait_ge(S["h"][p], i + 1)
                    sp.dma_start(x[0:rows_of(load), p], t["x_sample"] if is_sample(load) else
                                 t["x_prompt"][tile_rows(load), :]).then_inc(S["x"][p], 16)
                new = is_sample(n)
                rows = slice(0, NS) if new else tile_rows(n)
                sp.wait_ge(S["qkg"][p], i + 1)
                sp.dma_start(t["q"][tile_rows(n), :], qk[0:r, p, 0:AW]).then_inc(S["qks"][p], 16)
                sp.dma_start(t["k_new" if new else "k_prompt"][rows, :], qk[0:r, p, AW:2 * AW]).then_inc(S["qks"][p], 16)
                sp.wait_ge(S["ve"][p], i + 1)
                sp.dma_start(t["v_new" if new else "v_prompt"][rows, :], vu[0:r, p, 0:AW]).then_inc(S["vus"][p], 16)
                sp.wait_ge(S["ue"][p], i + 1)
                sp.dma_start(t["u"][tile_rows(n), :], vu[0:r, p, AW:D]).then_inc(S["vus"][p], 16)

            run_steps(sp, step, SECTIONS, 2)
            for p in range(2):
                turns = (TILES + 1 - p) // 2
                sp.wait_ge(S["qks"][p], 32 * turns)
                sp.wait_ge(S["vus"][p], 32 * turns)

        @block.scalar
        def _(act):
            def ahead(n):
                r, p, i = rows_of(n), n.slot(2), n.times(1, 2)
                act.wait_ge(S["x"][p], i * 16 + 16)
                act.activation(junk[0:r, :], x[0:r, p], ACT.Square, accum_out=ss[0:r, p, 0:1]).then_inc(s_act, 1)
                act.wait_ge(s_act, n.idx + 1)
                act.activation(ss[0:r, p, 1:2], ss[0:r, p, 0:1], ACT.Sqrt, scale=1.0 / D, bias=const["eps"][0:r, :]).then_inc(S["root"][p], 1)
                act.wait_ge(S["hTp"][p], i + 1)
                act.wait_ge(S["um"][p], i)
                act.activation(hT[:, p, 0:4, 0:r], hT_ps[:, 0:512].rearrange("p (k n) -> p k n", n=128)[:, :, 0:r], ACT.Copy).then_inc(S["hTa"][p], 1)

            def behind(n):
                r, p, i = rows_of(n), n.slot(2), n.times(1, 2)
                act.wait_ge(S["qkm"][p], i + 1)
                act.activation(sq[0:r, :], out_ps[0:r, 0:2 * AW], ACT.Square).then_inc(S["hsq"][p], 1)
                act.wait_ge(S["hss"][p], i + 1)
                act.activation(hss[0:r, p, 1, :], hss[0:r, p, 0, :], ACT.Sqrt, scale=1.0 / HD, bias=const["eps"][0:r, :]).then_inc(S["hroot"][p], 1)
                act.wait_ge(S["vm"][p], i + 1)
                act.wait_ge(S["vus"][p], i * 32)
                act.activation(vu[0:r, p, 0:AW], out_ps[0:r, D:D + AW], ACT.Copy).then_inc(S["ve"][p], 1)
                act.wait_ge(S["um"][p], i + 1)
                act.activation(vu[0:r, p, AW:D], out_ps[0:r, D + AW:2 * D], ACT.Copy).then_inc(S["ue"][p], 1)

            lookahead(act, ahead, behind, TILES, SECTIONS)

        @block.tensor
        def _(pe):
            pe.wait_ge(s_win, 32)

            def ahead(n):
                r, p, i = rows_of(n), n.slot(2), n.times(1, 2)
                pe.wait_ge(S["h"][p], i + 1)
                before = i + (1 if p == 1 else 0)
                pe.wait_ge(S["hTa"][1 - p], before)
                pe.wait_ge(S["hTd"][1 - p], before)
                for k in range(KT):
                    mm = pe.transpose(hT_ps[:, k * 128:k * 128 + r], h[0:r, p, k * 128:(k + 1) * 128], const["ident"][0:r, 0:r])
                mm.then_inc(S["hTp"][p], 1)

            def behind(n):
                r, p, i = rows_of(n), n.slot(2), n.times(1, 2)
                before = i + (1 if p == 1 else 0)
                pe.wait_ge(S["hTa"][p], i + 1)
                pe.wait_ge(S["hTd"][p], i + 1)
                for c in range(4):
                    pe.wait_ge(S[("qkn", "qkn", "ve", "ue")[c]][1 - p], before)
                    for k in range(KT):
                        mm = pe.matmul(out_ps[0:r, c * 512:(c + 1) * 512], hT[:, p, k, 0:r],
                                       w_in_sb[:, k, c * 512:(c + 1) * 512], start=(k == 0), stop=(k == KT - 1))
                    if c:
                        mm.then_inc(S[(None, "qkm", "vm", "um")[c]][p], 1)

            lookahead(pe, ahead, behind, TILES, SECTIONS)

        @block.vector
        def _(dve):
            dve.wait_ge(s_g, 16 * 7)
            for j, r in ((0, 128), (1, NS)):
                dve.scalar_tensor_tensor(A[0:r, j], A[0:r, j], 1.0, g1[0:r, :], ALU.add, ALU.mult).then_inc(s_A, 1)
            dve.wait_ge(s_A, 2)

            def behind(n):
                r, p, i = rows_of(n), n.slot(2), n.times(1, 2)
                dve.wait_ge(S["hsq"][p], i + 1)
                dve.tensor_reduce(hss[0:r, p, 0, :], sq[0:r, :].rearrange("p (a d) -> p a d", d=HD), AX.X, ALU.add).then_inc(S["hss"][p], 1)
                dve.wait_ge(S["hroot"][p], i + 1)
                dve.reciprocal(hss[0:r, p, 2, :], hss[0:r, p, 1, :]).then_inc(s_dve, 1)
                dve.wait_ge(s_dve, 3 * TILES if is_sample(n) else n.times(3) + 5)
                dve.wait_ge(S["qks"][p], i * 32)
                dve.tensor_tensor(qk[0:r, p].rearrange("p (a d) -> p a d", d=HD),
                                  out_ps[0:r, 0:2 * AW].rearrange("p (a d) -> p a d", d=HD),
                                  hss[0:r, p, 2, :].unsqueeze(2).broadcast_to([r, 2 * HEADS, HD]), ALU.mult).then_inc(S["qkn"][p], 1)

            def ahead(n):
                r, p, i = rows_of(n), n.slot(2), n.times(1, 2)
                j = 1 if is_sample(n) else 0
                c0 = 0 if n.i is None and n.add == 0 else n.times(3) - 1
                dve.wait_ge(S["root"][p], i + 1)
                dve.reciprocal(ss[0:r, p, 2:3], ss[0:r, p, 1:2]).then_inc(s_dve, 1)
                dve.wait_ge(s_dve, c0 + 1)
                dve.wait_ge(S["hTp"][p], i)
                dve.scalar_tensor_tensor(h[0:r, p], x[0:r, p], ss[0:r, p, 2:3], A[0:r, j], ALU.mult, ALU.mult).then_inc(s_dve, 1)
                dve.wait_ge(s_dve, c0 + 2)
                dve.tensor_tensor(h[0:r, p], h[0:r, p], B[0:r, j], ALU.add).then_inc(S["h"][p], 1)
                dve.wait_ge(S["hTp"][p], i + 1)
                dve.wait_ge(S["um"][p], i)
                dve.tensor_copy(hT[:, p, 4:8, 0:r], hT_ps[:, 512:1024].rearrange("p (k n) -> p k n", n=128)[:, :, 0:r]).then_inc(S["hTd"][p], 1)

            lookahead(dve, ahead, behind, TILES, SECTIONS)

        @block.gpsimd
        def _(pool):
            pool.wait_ge(s_g, 16 * 7)

            def step(n):
                r, p, i = rows_of(n), n.slot(2), n.times(1, 2)
                pool.wait_ge(S["qkn"][p], i + 1)
                v = qk[0:r, p].rearrange("p (j a d) -> p j a d", j=2, d=HD)
                g = gqk[0:r, :].rearrange("p (j d) -> p j d", j=2).unsqueeze(2).broadcast_to([r, 2, HEADS, HD])
                pool.tensor_tensor(v, v, g, ALU.mult).then_inc(S["qkg"][p], 1)

            run_steps(pool, step, SECTIONS, 2)


DILATIONS = ((2048, 16), (512, 4), (128, 1))
QB = 128
assert all(w // d == QB for w, d in DILATIONS)
NEG = -1e30
OROW = AW + 2 * HEADS


def attention_stage(nc, t, const):
    BLOCKS = SEQ // QB
    STEPS = BLOCKS * len(DILATIONS)
    SCALE = HD ** -0.5
    SECTIONS = ((0, 4, False), (4, 16, True), (16, 20, False), (20, 32, True), (32, 36, False),
                (36, 44, True), (44, 48, False))
    LOADS = ((0, 4, False), (4, 16, True), (16, 32, True), (32, 48, True))

    def has_prev(n):
        if n.add < BLOCKS:
            return False
        if n.add < 2 * BLOCKS:
            return n.add % 4 != 0
        return not (n.i is None and n.add == 2 * BLOCKS)

    def rows(a, n):
        pattern = n.add // BLOCKS
        d = DILATIONS[pattern][1]
        m = Turn(n.add - pattern * BLOCKS, n.i, n.mult)
        per_class = BLOCKS // d
        z, b = m.times(1, per_class) if per_class < BLOCKS else 0, m.add % per_class
        if pattern == 0:
            return a[0:SEQ, :].rearrange("(n d) c -> n d c", d=d)[:, bass.ds(m.idx, 1), :]
        if pattern == 1:
            return a[0:SEQ, :].rearrange("(b n d) c -> b n d c", d=d, b=per_class)[b, :, bass.ds(z, 1), :]
        return a[bass.ds(m.times(QB), QB), :].unsqueeze(1)

    with ExitStack() as ctx:
        P = Pool_(nc, ctx)
        mask = P.sb("a_mask", [128, 2 * QB])
        gate = P.sb("a_gate", [1, 1])
        q = P.sb("a_q", [128, 2, AW])
        k = P.sb("a_k", [128, 2, AW])
        v = P.sb("a_v", [128, 4, AW])
        qT = P.sb("a_qT", [128, 2, AW // 128, QB])
        kT = P.sb("a_kT", [128, 4, AW // 128, QB])
        pr = P.sb("a_probs", [128, 2, HEADS, 2 * QB])
        prT = P.sb("a_probsT", [128, 2, 2, 2 * QB])
        nb = P.sb("a_negmax", [128, 2, HEADS])
        o = P.sb("a_o", [128, 2, OROW])
        t_ps = P.ps("a_t_ps", [128, 512])
        s_ps = [[P.ps(f"a_s_ps{x}{y}", [128, 512]) for y in range(2)] for x in range(2)]
        p_ps = [P.ps(f"a_p_ps{x}", [128, 512]) for x in range(2)]
        o_ps = P.ps("a_o_ps", [128, 512])
        mask_made = P.sem("a_mask")
        qk_loaded, o_stored = P.sem2("a_qkl"), const["o_stored"]
        v_loaded = [P.sem(f"a_vl{x}") for x in range(4)]
        (qT_ps, kT_ps, qT_sb, kT_sb, scored, masked, negmax, exped, pT_ps, pT_dve, pT_act, pv_done, o_sb) = (
            P.sem("a_" + x) for x in ("qTp", "kTp", "qTs", "kTs", "sc", "mk", "nm", "ex", "pTp", "pTd", "pTa", "pv", "ob"))
        block = ctx.enter_context(nc.Block())

        @block.gpsimd
        def _(pool):
            pool.memset(mask[:, :], 0.0).then_inc(mask_made, 1)
            pool.wait_ge(mask_made, 1)
            pool.affine_select(out=mask[:, 0:QB], in_=mask[:, 0:QB], compare_op=ALU.is_ge, fill=NEG,
                               base=0, pattern=[[-1, QB]], channel_multiplier=1).then_inc(mask_made, 1)
            pool.affine_select(out=mask[:, QB:], in_=mask[:, QB:], compare_op=ALU.is_ge, fill=NEG,
                               base=0, pattern=[[1, QB]], channel_multiplier=-1).then_inc(mask_made, 1)

            def store(n):
                pool.wait_ge(o_sb, n.times(1) + 1)
                pool.dma_start(rows(t["o"][n.add // BLOCKS], n), o[:, n.slot(2)].unsqueeze(1)).then_inc(o_stored[n.slot(2)], 16)

            run_steps(pool, store, LOADS, 4)
            for p in range(2):
                pool.wait_ge(o_stored[p], 16 * STEPS // 2)

        @block.sync
        def _(sp):
            def step(n):
                p, r = n.slot(2), n.slot(4)
                wait(sp, kT_ps, n.times(1) - 1)
                sp.dma_start(q[:, p].unsqueeze(1), rows(t["q"], n)).then_inc(qk_loaded[p], 16)
                sp.dma_start(k[:, p].unsqueeze(1), rows(t["k_prompt"], n)).then_inc(qk_loaded[p], 16)
                wait(sp, pv_done, n.times(4) - 8)
                sp.dma_start(v[:, r].unsqueeze(1), rows(t["v_prompt"], n)).then_inc(v_loaded[r], 16)

            run_steps(sp, step, LOADS, 4)

        @block.scalar
        def _(act):
            def keys_out(n):
                act.wait_ge(kT_ps, n.times(1) + 1)
                wait(act, scored, n.times(2) - 4)
                act.activation(kT[:, n.slot(4)].rearrange("p k n -> p (k n)"), t_ps[:, :], ACT.Copy).then_inc(kT_sb, 1)

            def probs_out(n, pair):
                act.wait_ge(pT_ps, n.times(4) + pair + 1)
                wait(act, pv_done, n.times(4) + pair - 1)
                act.activation(prT[:, 1].rearrange("p a b -> p (a b)") if has_prev(n) else prT[:, 1, :, 0:QB],
                               p_ps[1][:, :] if has_prev(n) else p_ps[1][:, :].rearrange("p (a b) -> p a b", a=2)[:, :, 0:QB],
                               ACT.Copy).then_inc(pT_act, 1)

            def exps(n, quad):
                p, w = n.slot(2), 2 * QB if has_prev(n) else QB
                act.wait_ge(negmax, n.times(2) + quad + 1)
                for hd in range(4 * quad, 4 * quad + 4):
                    e = act.activation(pr[:, p, hd, 0:w], pr[:, p, hd, 0:w], ACT.Exp, scale=SCALE, bias=nb[:, p, hd:hd + 1],
                                       accum_out=o[:, p, AW + HEADS + hd:AW + HEADS + hd + 1])
                e.then_inc(exped, 1)

            def step(n):
                first, last = n.i is None and n.add == 0, n.i is None and n.add == STEPS - 1
                if not first:
                    probs_out(n + -1, 1)
                if not last:
                    keys_out(n + 1)
                if not first:
                    probs_out(n + -1, 3)
                exps(n, 0)
                exps(n, 1)

            keys_out(Turn(0))
            run_steps(act, step, SECTIONS, 4)
            for pair in (1, 3):
                probs_out(Turn(STEPS - 1), pair)

        @block.tensor
        def _(pe):
            def transpose_block(n, src, done, other, before):
                wait(pe, other, before)
                for j in range(AW // 128):
                    mm = pe.transpose(t_ps[:, j * QB:(j + 1) * QB], src[:, n.slot(2), j * 128:(j + 1) * 128], const["ident"][:, :])
                mm.then_inc(done, 1)

            def queries(n):
                pe.wait_ge(qk_loaded[n.slot(2)], n.times(32, 2) + 32)
                transpose_block(n, q, qT_ps, kT_sb, n.times(1))

            def keys(n):
                transpose_block(n, k, kT_ps, qT_sb, n.times(1) + 1)

            def scores(n, quad):
                pe.wait_ge(qT_sb, n.times(1) + 1)
                pe.wait_ge(kT_sb, n.times(1) + 1)
                wait(pe, masked, n.times(2) + quad - 1)
                for j in range(4):
                    hd = 4 * quad + j
                    lo, pair = HD * (hd % 2), hd // 2
                    bank = s_ps[quad][hd % 2]
                    at = (j // 2) * 2 * QB
                    for prev in range(2 if has_prev(n) else 1):
                        mm = pe.matmul(bank[:, at + prev * QB:at + (prev + 1) * QB], qT[lo:lo + HD, n.slot(2), pair, :],
                                       kT[lo:lo + HD, (n + -prev).add % 4, pair, :], start=True, stop=True)
                mm.then_inc(scored, 1)

            def probs(n, pair):
                pe.wait_ge(exped, n.times(2) + pair // 2 + 1)
                wait(pe, (pT_dve, pT_act)[pair % 2], n.times(2) + pair // 2)
                for x in range(2):
                    for prev in range(2 if has_prev(n) else 1):
                        at = x * 2 * QB + prev * QB
                        mm = pe.transpose(p_ps[pair % 2][:, at:at + QB], pr[:, n.slot(2), 2 * pair + x, prev * QB:(prev + 1) * QB],
                                          const["ident"][:, :])
                mm.then_inc(pT_ps, 1)

            def values(n, pair):
                pe.wait_ge((pT_dve, pT_act)[pair % 2], n.times(2) + pair // 2 + 1)
                if pair == 0:
                    pe.wait_ge(v_loaded[n.slot(4)], n.times(16, 4) + 16)
                    wait(pe, o_sb, n.times(1))
                for x in range(2):
                    hd = 2 * pair + x
                    last = 1 if has_prev(n) else 0
                    for prev in range(last + 1):
                        mm = pe.matmul(o_ps[:, hd * HD:(hd + 1) * HD], prT[:, pair % 2, x, prev * QB:(prev + 1) * QB],
                                       v[:, (n + -prev).add % 4, hd * HD:(hd + 1) * HD], start=(prev == 0), stop=(prev == last))
                mm.then_inc(pv_done, 1)

            def step(n):
                first, last = n.i is None and n.add == 0, n.i is None and n.add == STEPS - 1
                for quad in range(2):
                    if not last:
                        (queries, keys)[quad](n + 1)
                    if not first:
                        probs(n + -1, 2 * quad)
                        probs(n + -1, 2 * quad + 1)
                    scores(n, quad)
                    if not first:
                        values(n + -1, 2 * quad)
                        values(n + -1, 2 * quad + 1)

            queries(Turn(0))
            keys(Turn(0))
            run_steps(pe, step, SECTIONS, 4)
            for quad in range(2):
                for f in (probs, values):
                    for pair in (2 * quad, 2 * quad + 1):
                        f(Turn(STEPS - 1), pair)

        @block.vector
        def _(dve):
            dve.wait_ge(mask_made, 3)

            def queries_out(n):
                dve.wait_ge(qT_ps, n.times(1) + 1)
                wait(dve, scored, n.times(2) - 2)
                dve.tensor_copy(qT[:, n.slot(2)].rearrange("p k n -> p (k n)"), t_ps[:, :]).then_inc(qT_sb, 1)

            def maxima(n, quad):
                p, w = n.slot(2), 2 * QB if has_prev(n) else QB
                dve.wait_ge(scored, n.times(2) + quad + 1)
                if quad == 0:
                    wait(dve, pT_ps, n.times(4) - 4)
                    wait(dve, o_stored[p], n.times(16, 2))
                dve.memset(gate[:, :], 0.0)
                for j in range(4):
                    hd = 4 * quad + j
                    at = (j // 2) * 2 * QB
                    mx = dve.tensor_tensor_reduce(pr[:, p, hd, 0:w], s_ps[quad][hd % 2][:, at:at + w], mask[:, 0:w],
                                                  1.0, -3e38, ALU.add, ALU.max, o[:, p, AW + hd:AW + hd + 1])
                mx.then_inc(masked, 1)
                dve.wait_ge(masked, n.times(2) + quad + 1)
                dve.tensor_scalar(nb[:, p, 4 * quad:4 * quad + 4], o[:, p, AW + 4 * quad:AW + 4 * quad + 4], -SCALE, None,
                                  ALU.mult).then_inc(negmax, 1)

            def probs_out(n, pair):
                dve.wait_ge(pT_ps, n.times(4) + pair + 1)
                wait(dve, pv_done, n.times(4) + pair - 1)
                dve.tensor_copy(prT[:, 0].rearrange("p a b -> p (a b)") if has_prev(n) else prT[:, 0, :, 0:QB],
                                p_ps[0][:, :] if has_prev(n) else p_ps[0][:, :].rearrange("p (a b) -> p a b", a=2)[:, :, 0:QB]
                                ).then_inc(pT_dve, 1)

            def outputs_out(n):
                dve.wait_ge(pv_done, n.times(4) + 4)
                dve.tensor_copy(o[:, n.slot(2), 0:AW], o_ps[:, :]).then_inc(o_sb, 1)

            def step(n):
                first, last = n.i is None and n.add == 0, n.i is None and n.add == STEPS - 1
                if not last:
                    queries_out(n + 1)
                for quad in range(2):
                    if not first:
                        probs_out(n + -1, 2 * quad)
                    maxima(n, quad)
                if not first:
                    outputs_out(n + -1)

            queries_out(Turn(0))
            run_steps(dve, step, SECTIONS, 4)
            probs_out(Turn(STEPS - 1), 0)
            probs_out(Turn(STEPS - 1), 2)
            outputs_out(Turn(STEPS - 1))


LC = 8
GB = 8
BLKS = GROUPS // GB
NCH = SEQ // LC
HALF = NCH // 128
Z_W, Z_M, Z_C, Z_CJ, Z_T = 0, 2 * GB * 128, 3 * GB * 128, 4 * GB * 128, 5 * GB * 128
Z_COLS = Z_T + 2 * GB * NCH
TWO_PI_HI = 6.28125
TWO_PI_LO = 2 * math.pi - TWO_PI_HI
ROUND = 1.5 * 2.0 ** 23


def bc(ap, shape):
    return ap.broadcast_to(shape)


def state_space_constants_stage(nc, t, const, keep):
    with ExitStack() as ctx:
        P = Pool_(nc, ctx)
        prm = P.sb("z_prm", [GROUPS, 4, ST])
        cin = P.sb("z_cin", [128, BLKS, 4, ST])
        din = P.sb("z_din", [GROUPS, LC, CH])
        dsk = P.sb("z_dskip", [128, GROUPS])
        bA = P.sb("z_bA", [128, GROUPS, CH])
        bJ = P.sb("z_bJ", [128, GROUPS, CH])
        sm = P.sb("z_small", [128, 24, GROUPS])
        bbA = P.sb("z_bbA", [128, GROUPS, CH])
        bbJ = P.sb("z_bbJ", [128, GROUPS, CH])
        b1 = P.sb("z_b1", [128, GROUPS, CH])
        b2 = P.sb("z_b2", [128, GROUPS, CH])
        cA = P.sb("z_cA", [128, GROUPS, CH])
        cJ = P.sb("z_cJ", [128, GROUPS, CH])
        pad = P.sb("z_pad", [128, GB, 2 * LC - 1, CH])
        dblk = P.sb("z_dblk", [128, GB])
        wA = P.sb("z_wA", [128, GB, LC, CH])
        wJ = P.sb("z_wJ", [128, GB, LC, CH])
        t1 = P.sb("z_t1", [128, GB, LC + 1, CH])
        t2 = P.sb("z_t2", [128, GB, LC + 1, CH])
        cm = P.sb("z_cm", [128, GB, LC + 1, CH])
        cmJ = P.sb("z_cmJ", [128, GB, LC, CH])
        wT = P.sb("z_wT", [128, 2, GB, 128])
        m_sb = P.sb("z_m", [128, GB, 128])
        tab = P.sb("z_tab", [128, 2, GB, NCH])
        tt = P.sb("z_tt", [128, 4, GB, NCH // 2])
        em = P.sb("z_em", [128, 2, 3, GB])
        gate = P.sb("z_gate", [1, 2])
        psT = P.ps("z_psT", [128, 4 * 512])
        psM = P.ps("z_psM", [128, 2 * 512])
        psP = P.ps("z_psP", [128, 512])
        (d_prm, d_b, d_c, d_zw, d_zm, d_zc, d_zt, s_dt, s_rho, s_th, s_sin, s_prmT, s_cT, s_dve, s_pool,
         s_small, s_w, s_wT, s_wT_out, s_pad, s_mp, s_m, s_cm, s_tab, s_aps) = (P.sem("z_" + x) for x in (
             "dprm", "db", "dc", "dzw", "dzm", "dzc", "dzt", "dt", "rho", "th", "sin", "prmT", "cT", "dve", "pool",
             "small", "w", "wT", "wTo", "pad", "mp", "m", "cm", "tab", "aps"))
        (ARE, AIM, LDT, TRE, TH, K, R, SIN, SINH, COS, A1R, A1I, RHO, DEN, F1, F2, FR, FI, E8R, E8I, X1, X2, DT, NR) = range(24)
        pw = keep["pw"]
        pwR = P.sb("z_pwR", [128, 2, GROUPS, LC])
        rho8 = keep["rho8"]
        sgn, nsgn = keep["sgn"], keep["nsgn"]
        z = t["zc"]
        block = ctx.enter_context(nc.Block())

        @block.sync
        def _(sp):
            for j, name in enumerate(("ssm_a_re", "ssm_a_re", "ssm_a_im", "ssm_a_im")):
                sp.dma_start(prm[:, j, :], t[name]).then_inc(d_prm, 16)
            sp.dma_start(sm[:, LDT, :], t["ssm_log_dt"].rearrange("(o n) -> o n", o=1).broadcast_to([128, GROUPS])).then_inc(d_prm, 16)
            for j, (top, bottom) in enumerate((("ssm_b_re", "ssm_b_im"), ("ssm_b_im", "ssm_b_re"))):
                for part, name in enumerate((top, bottom)):
                    sp.dma_start((bA, bJ)[j][part * ST:(part + 1) * ST], t[name].rearrange("g n c -> n g c")).then_inc(d_b, 16)
            for j, name in enumerate(("ssm_c_re", "ssm_c_im", "ssm_c_im", "ssm_c_re")):
                sp.dma_start(cin[:, :, j, :], t[name].rearrange("(b g) c n -> (g c) b n", b=BLKS)).then_inc(d_c, 16)
            for j in range(LC):
                sp.dma_start(din[:, j, :], t["ssm_d"].rearrange("(g c) -> g c", c=CH)).then_inc(d_prm, 16)
            for i in range(BLKS):
                zb = z[i]
                sp.wait_ge(s_cm, i * 2 + 2)
                sp.dma_start(zb[:, Z_C:Z_CJ].rearrange("p (g x) -> p g x", g=GB), cm[:, :, 1:, :].rearrange("p g j c -> p g (j c)")).then_inc(d_zc, 16)
                sp.dma_start(zb[:, Z_CJ:Z_T], cmJ[:, :, :, :].rearrange("p g j c -> p (g j c)")).then_inc(d_zc, 16)
                sp.wait_ge(s_wT_out, i * 2 + 2)
                sp.dma_start(zb[:, Z_W:Z_M], wT[:, :, :, :].rearrange("p a g c -> p (a g c)")).then_inc(d_zw, 16)
                sp.wait_ge(s_m, i + 1)
                sp.dma_start(zb[:, Z_M:Z_C], m_sb[:, :, :].rearrange("p g c -> p (g c)")).then_inc(d_zm, 16)
                sp.wait_ge(s_tab, i + 1)
                sp.dma_start(zb[:, Z_T:Z_COLS], tab[:, :, :, :].rearrange("p a g c -> p (a g c)")).then_inc(d_zt, 16)
            sp.wait_ge(d_zc, 32 * BLKS)
            for d in (d_zw, d_zm, d_zt):
                sp.wait_ge(d, 16 * BLKS)

        @block.scalar
        def _(act):
            act.wait_ge(d_prm, 16 * (5 + LC))
            act.activation(sm[:, DT, :], sm[:, LDT, :], ACT.Exp).then_inc(s_dt, 1)
            act.wait_ge(s_th, 1)
            act.activation(sm[:, RHO, :], sm[:, TRE, :], ACT.Exp).then_inc(s_rho, 1)
            act.activation(rho8[:, :], sm[:, TRE, :], ACT.Exp, scale=float(LC)).then_inc(s_rho, 1)
            act.wait_ge(s_th, 2)
            act.activation(sm[:, SIN, :], sm[:, R, :], ACT.Sin).then_inc(s_sin, 1)
            act.activation(sm[:, SINH, :], sm[:, R, :], ACT.Sin, scale=0.5).then_inc(s_sin, 1)
            with act.Fori(0, BLKS) as i:
                act.wait_ge(d_zw, i * 16)
                for a in range(2):
                    act.wait_ge(s_wT, i * 2 + a + 1)
                    act.activation(wT[:, a].rearrange("p g c -> p (g c)"), psT[:, a * D:(a + 1) * D], ACT.Copy).then_inc(s_wT_out, 1)

        @block.tensor
        def _(pe):
            pe.wait_ge(d_prm, 16 * (5 + LC))
            pe.transpose(psP[:, 2 * GROUPS:3 * GROUPS], din[:, :, :].rearrange("g s c -> g (s c)"), const["ident"][0:GROUPS, 0:GROUPS])
            for a in range(2):
                mm = pe.transpose(psP[:, a * GROUPS:(a + 1) * GROUPS], prm[:, 2 * a:2 * a + 2, :].rearrange("p a n -> p (a n)"),
                                  const["ident"][0:GROUPS, 0:GROUPS])
            mm.then_inc(s_prmT, 1)
            pe.wait_ge(d_c, 16 * 4)
            for b in range(BLKS):
                for a in range(2):
                    mm = pe.transpose(psM[:, a * 512 + b * 128:a * 512 + (b + 1) * 128],
                                      cin[:, b, 2 * a:2 * a + 2, :].rearrange("p a n -> p (a n)"), const["ident"][:, :])
            mm.then_inc(s_cT, 1)
            with pe.Fori(0, BLKS) as i:
                pe.wait_ge(s_wT_out, i * 2)
                for a, w in enumerate((wA, wJ)):
                    pe.wait_ge(s_w, i * 2 + a + 1)
                    for g in range(GB):
                        mm = pe.transpose(psT[:, (a * GB + g) * 128:(a * GB + g + 1) * 128], w[:, g].rearrange("p s c -> p (s c)"),
                                          const["ident"][:, :])
                    mm.then_inc(s_wT, 1)
                pe.wait_ge(s_cm, i * 2 + 1)
                pe.wait_ge(s_pad, i + 1)
                pe.wait_ge(s_m, i)
                pe.wait_ge(s_cT, 1)
                pe.wait_ge(s_small, 1)
                for g in range(GB):
                    for s in range(LC):
                        mm = pe.matmul(psM[:, g * 128 + s * CH:(g + 1) * 128],
                                       pad[:, g, LC - 1 - s:2 * LC - 1 - s, :].rearrange("p s c -> p (s c)"),
                                       cm[:, g, 0:LC - s, :].rearrange("p s c -> p (s c)"), start=(s == 0), stop=(s == LC - 1))
                mm.then_inc(s_mp, 1)

        @block.gpsimd
        def _(pool):
            pool.wait_ge(s_small, 1)
            with pool.Fori(0, BLKS) as i:
                st = Steps(pool, s_pool, i * POOL_STEPS)
                pool.wait_ge(d_zt, i * 16)
                pool.tensor_tensor(gate[:, 1:], const["eps"][0:1, :], const["eps"][0:1, :], ALU.mult)
                for a in range(2):
                    pool.tensor_copy(em[:, 0, a, :], keep["e8"][:, a, bass.ds(i * GB, GB)])
                    st.did(pool.memset(tab[:, a, :, 0:1], 1.0 - a))
                st.wait()
                m, cur = 1, 0
                while m < NCH:
                    er, ei = (bc(em[:, cur, a, :].unsqueeze(2), [128, GB, m]) for a in range(2))
                    c, s = tab[:, 0, :, 0:m], tab[:, 1, :, 0:m]
                    q = [tt[:, j, :, 0:m] for j in range(4)]
                    for j, (x, e) in enumerate(((c, er), (s, ei), (c, ei), (s, er))):
                        last = pool.tensor_tensor(q[j], x, e, ALU.mult)
                    st.link(last)
                    pool.tensor_tensor(tab[:, 0, :, m:2 * m], q[0], q[1], ALU.subtract)
                    last = pool.tensor_tensor(tab[:, 1, :, m:2 * m], q[2], q[3], ALU.add)
                    if 2 * m < NCH:
                        a, b = em[:, cur, 0, :], em[:, cur, 1, :]
                        st.link(last)
                        w = [tt[:, j, :, 0] for j in range(3)]
                        pool.tensor_tensor(w[0], a, a, ALU.mult)
                        pool.tensor_tensor(w[1], b, b, ALU.mult)
                        st.link(pool.tensor_tensor(w[2], a, b, ALU.mult))
                        pool.tensor_tensor(em[:, 1 - cur, 0, :], w[0], w[1], ALU.subtract)
                        st.link(pool.tensor_tensor(em[:, 1 - cur, 1, :], w[2], w[2], ALU.add))
                    else:
                        last.then_inc(s_tab, 1)
                    m, cur = 2 * m, 1 - cur
                assert st.n == POOL_STEPS, st.n

        @block.vector
        def _(dve):
            st = Steps(dve, s_dve)
            x = lambda j: sm[:, j, :]
            mul = lambda o, a, b: dve.tensor_tensor(o, a, b, ALU.mult)
            add = lambda o, a, b: dve.tensor_tensor(o, a, b, ALU.add)
            sub = lambda o, a, b: dve.tensor_tensor(o, a, b, ALU.subtract)
            dve.memset(pad[:, :, :, :], 0.0)
            dve.memset(pw[:, 0, :, 0:1], 1.0)
            dve.memset(pw[:, 1, :, 0:1], 0.0)
            dve.wait_ge(s_prmT, 1)
            st.link(dve.tensor_copy(sm[:, ARE:AIM + 1, :], psP[:, 0:2 * GROUPS].rearrange("p (a g) -> p a g", a=2)))
            dve.tensor_copy(dsk[:, :], psP[:, 2 * GROUPS:3 * GROUPS])
            dve.wait_ge(s_dt, 1)
            mul(x(TRE), x(DT), x(ARE)).then_inc(s_th, 1)
            st.link(mul(x(TH), x(DT), x(AIM)))
            st.link(dve.tensor_scalar(x(X1), x(TH), 1.0 / (2 * math.pi), ROUND, ALU.mult, ALU.add))
            st.link(dve.tensor_scalar(x(K), x(X1), -ROUND, None, ALU.add))
            st.link(dve.scalar_tensor_tensor(x(X1), x(K), -TWO_PI_HI, x(TH), ALU.mult, ALU.add))
            st.link(dve.scalar_tensor_tensor(x(X2), x(K), -TWO_PI_LO, x(X1), ALU.mult, ALU.add))
            dve.tensor_scalar(x(R), x(X2), 3.1415925, -3.1415925, ALU.min, ALU.max).then_inc(s_th, 1)
            mul(x(F1), x(ARE), x(ARE))
            st.link(mul(x(F2), x(AIM), x(AIM)))
            st.link(add(x(DEN), x(F1), x(F2)))
            dve.wait_ge(s_sin, 2)
            dve.wait_ge(s_rho, 2)
            st.link(mul(x(X1), x(SINH), x(SINH)))
            st.link(dve.tensor_scalar(x(COS), x(X1), -2.0, 1.0, ALU.mult, ALU.add))
            mul(x(A1R), x(RHO), x(COS))
            st.link(mul(x(A1I), x(RHO), x(SIN)))
            dve.tensor_scalar(x(NR), x(A1R), -1.0, None, ALU.add)
            dve.tensor_copy(pw[:, 0, :, 1], x(A1R))
            st.link(dve.tensor_copy(pw[:, 1, :, 1], x(A1I)))
            mul(x(F1), x(NR), x(ARE))
            mul(x(F2), x(A1I), x(AIM))
            dve.reciprocal(x(X2), x(DEN))
            mul(x(K), x(A1I), x(ARE))
            st.link(mul(x(R), x(NR), x(AIM)))
            add(x(F1), x(F1), x(F2))
            st.link(sub(x(K), x(K), x(R)))
            mul(x(FR), x(F1), x(X2))
            st.link(mul(x(FI), x(K), x(X2)))

            def cmul(outr, outi, ar, ai, br, bi, q):
                mul(q[0], ar, br)
                mul(q[1], ai, bi)
                mul(q[2], ar, bi)
                st.link(mul(q[3], ai, br))
                sub(outr, q[0], q[1])
                st.link(add(outi, q[2], q[3]))

            for m in (1, 2, 4):
                n = [GROUPS, m]
                q = [v[:, :, 0:m] for v in (b1, b2, bbA, bbJ)]
                cmul(pw[:, 0, :, m + 1:2 * m + 1], pw[:, 1, :, m + 1:2 * m + 1], pw[:, 0, :, 1:m + 1], pw[:, 1, :, 1:m + 1],
                     bc(pw[:, 0, :, m:m + 1], [128] + n), bc(pw[:, 1, :, m:m + 1], [128] + n), q)
            for s in range(LC):
                dve.tensor_copy(pwR[:, :, :, s], pw[:, :, :, LC - 1 - s])
            q = [v[:, :, 0] for v in (b1, b2, bbA, bbJ)]
            cmul(x(E8R), x(E8I), x(COS), x(SIN), x(COS), x(SIN), q)
            cmul(x(X1), x(X2), x(E8R), x(E8I), x(E8R), x(E8I), q)
            cmul(keep["e8"][:, 0, :], keep["e8"][:, 1, :], x(X1), x(X2), x(X1), x(X2), q)
            dve.wait_ge(d_b, 16 * 4)
            st.link(dve.tensor_scalar(bJ[:, :, :], bJ[:, :, :], nsgn[:, :], None, ALU.mult))
            fr, fi = (bc(x(j).unsqueeze(2), [128, GROUPS, CH]) for j in (FR, FI))
            mul(b1[:, :, :], fr, bA[:, :, :])
            st.link(mul(b2[:, :, :], fi, bJ[:, :, :]))
            st.link(add(bbA[:, :, :], b1[:, :, :], b2[:, :, :]))
            mul(b1[:, :, :], fr, bJ[:, :, :])
            st.link(mul(b2[:, :, :], fi, bA[:, :, :]))
            st.link(sub(bbJ[:, :, :], b1[:, :, :], b2[:, :, :]))
            dve.wait_ge(s_cT, 1)
            dve.tensor_scalar(cA[:, :, :].rearrange("p g c -> p (g c)"), psM[:, 0:512], sgn[:, :], None, ALU.mult)
            dve.tensor_scalar(cJ[:, :, :].rearrange("p g c -> p (g c)"), psM[:, 512:1024], -1.0, None, ALU.mult).then_inc(s_small, 1)
            dve.wait_ge(s_small, 1)
            base = st.n
            with dve.Fori(0, BLKS) as i:
                st = Steps(dve, s_dve, i * DVE_STEPS + base)
                g0 = bass.ds(i * GB, GB)
                pr, pi = (bc(pwR[:, a, g0, :].unsqueeze(3), [128, GB, LC, CH]) for a in range(2))
                xA, xJ = (bc(v[:, g0, :].unsqueeze(2), [128, GB, LC, CH]) for v in (bbA, bbJ))
                u1, u2 = t1[:, :, 0:LC, :], t2[:, :, 0:LC, :]
                dve.wait_ge(s_wT, i * 2)
                mul(u1, pr, xA)
                st.link(mul(u2, pi, xJ))
                add(wA[:, :, :, :], u1, u2).then_inc(s_w, 1)
                dve.wait_ge(s_w, i * 2 + 1)
                mul(u1, pr, xJ)
                st.link(mul(u2, pi, xA))
                sub(wJ[:, :, :, :], u1, u2).then_inc(s_w, 1)
                dve.wait_ge(s_w, i * 2 + 2)
                pr, pi = (bc(pw[:, a, g0, :].unsqueeze(3), [128, GB, LC + 1, CH]) for a in range(2))
                yA, yJ = (bc(v[:, g0, :].unsqueeze(2), [128, GB, LC + 1, CH]) for v in (cA, cJ))
                mul(t1[:, :, :, :], pr, yA)
                st.link(mul(t2[:, :, :, :], pi, yJ))
                dve.wait_ge(d_zc, i * 32)
                dve.wait_ge(s_mp, i)
                add(cm[:, :, :, :], t1[:, :, :, :], t2[:, :, :, :]).then_inc(s_cm, 1)
                dve.wait_ge(s_cm, i * 2 + 1)
                mul(u1, pr[:, :, 1:, :], yJ[:, :, 1:, :])
                st.link(mul(u2, pi[:, :, 1:, :], yA[:, :, 1:, :]))
                sub(cmJ[:, :, :, :], u1, u2).then_inc(s_cm, 1)
                dve.wait_ge(s_cm, i * 2 + 2)
                dve.memset(gate[:, 0:1], 0.0)
                dve.tensor_copy(pad[:, :, LC - 1, :], bbA[:, g0, :]).then_inc(s_pad, 1)
                st.link(dve.tensor_copy(dblk[:, :], dsk[:, g0]))
                dve.wait_ge(s_mp, i + 1)
                dve.wait_ge(d_zm, i * 16)
                for g in range(GB):
                    last = dve.scalar_tensor_tensor(m_sb[:, g, :], const["ident"][:, :], dblk[:, g:g + 1], psM[:, g * 128:(g + 1) * 128],
                                                    ALU.mult, ALU.add)
                last.then_inc(s_m, 1)
                assert st.n == DVE_STEPS, st.n


POOL_STEPS = 2 + 8 + 7 * 3
DVE_STEPS = 5


def state_space_stage(nc, t, const, keep):
    with ExitStack() as ctx:
        P = Pool_(nc, ctx)
        zc = P.sb("y_zc", [128, 2, Z_COLS])
        u = P.sb("y_u", [128, HALF, LC, 128])
        uS = P.sb("y_uS", [NB, LC, 128])
        ug = P.sb("y_ug", [128, HALF, GB, LC, CH])
        uSg = P.sb("y_uSg", [NB, GB, LC, CH])
        hin = P.sb("y_hin", [NB * GB, 4, ST])
        uT = P.sb("y_uT", [128, GB, NCH])
        uTS = P.sb("y_uTS", [128, GB, NB])
        g1 = P.sb("y_g1", [128, 2, NCH])
        g2 = P.sb("y_g2", [128, 2, NCH])
        G = P.sb("y_G", [128, 2, NCH])
        H = P.sb("y_H", [128, 2, 2, NCH + 1])
        fin = P.sb("y_fin", [128, 2, GB])
        finT = P.sb("y_finT", [GB, 128])
        y = P.sb("y_y", [128, HALF, LC, 128])
        yS = P.sb("y_yS", [NB, TS, 128])
        h0 = P.sb("y_h0", [128, 2, GB, NB])
        ha = P.sb("y_ha", [128, 2, GB, NB])
        hl = P.sb("y_hl", [128, NB, GB])
        hsT = P.sb("y_hsT", [NB * GB, 128])
        rho = P.sb("y_rho", [128, GB])
        p4 = P.sb("y_p4", [128, 2, GB])
        gate = P.sb("y_gate", [1, 1])
        ps_u = P.ps("y_ps_u", [128, 2048])
        ps_v = [P.ps(f"y_ps_v{x}", [128, 512]) for x in range(2)]
        ps_y = [P.ps(f"y_ps_y{x}", [128, 512]) for x in range(2)]
        d_zc = P.sem2("y_dzc")
        (d_u, d_h, d_y, d_f, zeroed, uTp, uTa, uTd, uSs, v_ps, gmul, gsum, scanned, turned, yp, ya, s_blk, finp, fino,
         h0s, hsp, hso, s_dve, s_pe_hs, grouped) = (P.sem("y_" + x) for x in (
             "du", "dh", "dy", "df", "zero", "uTp", "uTa", "uTd", "uSs", "vp", "gm", "gs", "sc", "tu", "yp", "ya", "blk", "fp", "fo",
             "h0s", "hsp", "hso", "dve", "peh", "gr"))
        block = ctx.enter_context(nc.Block())
        up = t["u"][0:SEQ, :].rearrange("(h k s) c -> k h s c", h=HALF, s=LC)
        us = t["u"][SEQ:ROWS, :].rearrange("(b s) c -> b s c", s=TS)
        yp_d = t["y"][0:SEQ, :].rearrange("(h k s) c -> k h s c", h=HALF, s=LC)
        ys_d = t["y"][SEQ:ROWS, :].rearrange("(b s) c -> b s c", s=TS)
        SECTIONS = ((0, BLKS, True),)

        @block.sync
        def _(sp):
            def constants_in(n):
                sp.dma_start(zc[:, n.slot(2)].unsqueeze(1), t["zc"].rearrange("b p x -> p b x")[:, bass.ds(n.idx, 1), :]).then_inc(d_zc[n.slot(2)], 16)

            def step(n):
                cols = bass.ds(n.times(128), 128)
                wait(sp, yp, n.times(GB) - GB)
                constants_in(n)
                wait(sp, grouped, n.times(1))
                for h in range(HALF):
                    sp.dma_start(u[:, h], up[:, h, :, cols]).then_inc(d_u, 16)
                sp.dma_start(uS[:, TS:, :], us[:, :, cols]).then_inc(d_u, 16)
                wait(sp, uTp, n.times(1))
                for j, name in enumerate(("state_ssm_re", "state_ssm_im", "state_ssm_im", "state_ssm_re")):
                    for b in range(NB):
                        sp.dma_start(hin[b * GB:(b + 1) * GB, j, :], t[name][b, bass.ds(n.times(GB), GB), :]).then_inc(d_h, 16)

            step(Turn(0))
            step(Turn(1))
            run_steps(sp, step, ((2, BLKS, True),), 2)

        @block.gpsimd
        def _(pool):
            pool.memset(uSg[:, :, 0:TS, :], 0.0)
            pool.memset(H[:, :, :, 0:1], 0.0).then_inc(zeroed, 1)

            def step(n):
                tabs = zc[:, n.slot(2), Z_T:Z_COLS].rearrange("p (a g k) -> p a g k", a=2, g=GB)
                pool.wait_ge(d_zc[n.slot(2)], n.times(16, 2) + 16)
                for g in range(GB):
                    q, at = g % 2, n.times(GB) + g
                    pool.wait_ge(scanned, at + 1)
                    wait(pool, yp, at - (g > 0))
                    if g == 0:
                        wait(pool, finp, n.times(1))
                    last = pool.tensor_tensor(fin[:, :, g:g + 1], tabs[:, :, g, NCH - 1:NCH],
                                              bc(G[:, q, NCH - 1:NCH].unsqueeze(1), [128, 2, 1]), ALU.mult)
                    if g == GB - 1:
                        last.then_inc(s_blk, 1)
                    pool.tensor_tensor(H[:, q, 0, 1:], tabs[:, 0, g, :], G[:, q, :], ALU.mult)
                    pool.tensor_tensor(H[:, q, 1, 1:], tabs[:, 1, g, :], G[:, q, :], ALU.mult).then_inc(turned, 1)

            run_steps(pool, step, SECTIONS, 2)

        @block.scalar
        def _(act):
            act.wait_ge(zeroed, 1)

            def step(n):
                cols = bass.ds(n.times(128), 128)
                wait(act, uTp, n.times(1))
                act.wait_ge(d_u, n.times(48) + 48)
                for h in range(HALF):
                    act.activation(ug[:, h].rearrange("p g s c -> p s g c"), u[:, h].rearrange("p s (g c) -> p s g c", g=GB), ACT.Copy)
                act.activation(uSg[:, :, TS:, :].rearrange("p g s c -> p s g c"),
                               uS[:, TS:, :].rearrange("p s (g c) -> p s g c", g=GB), ACT.Copy).then_inc(grouped, 1)
                act.wait_ge(uTp, n.times(1) + 1)
                wait(act, yp, n.times(GB))
                act.activation(uT[:, 0:4, :].rearrange("p g k -> p (g k)"), ps_u[:, 0:1024], ACT.Copy).then_inc(uTa, 1)
                act.wait_ge(d_y, n.times(48))
                for g in range(GB):
                    act.wait_ge(yp, n.times(GB) + g + 1)
                    ps = ps_y[g % 2]
                    act.activation(y[:, :, :, g * CH:(g + 1) * CH], ps[:, 0:256].rearrange("p (h s c) -> p h s c", h=HALF, s=LC), ACT.Gelu_apprx_tanh)
                    act.activation(yS[:, :, g * CH:(g + 1) * CH], ps[0:NB, 256:256 + TS * CH].rearrange("p (s c) -> p s c", s=TS),
                                   ACT.Gelu_apprx_tanh).then_inc(ya, 1)
                act.wait_ge(ya, n.times(GB) + GB)
                for h in range(HALF):
                    act.dma_start(yp_d[:, h, :, cols], y[:, h]).then_inc(d_y, 16)
                act.dma_start(ys_d[:, :, cols], yS[:, :, :]).then_inc(d_y, 16)
                rows = bass.ds(n.times(GB), GB)
                act.wait_ge(fino, n.times(1) + 1)
                act.dma_start(t["ssm_re_prompt"][rows, :], finT[:, 0:ST]).then_inc(d_f, 16)
                act.dma_start(t["ssm_im_prompt"][rows, :], finT[:, ST:]).then_inc(d_f, 16)
                act.wait_ge(hso, n.times(1) + 1)
                for j, name in enumerate(("ssm_re_sample", "ssm_im_sample")):
                    for b in range(NB):
                        act.dma_start(t[name][b, rows, :], hsT[b * GB:(b + 1) * GB, j * ST:(j + 1) * ST]).then_inc(d_f, 16)

            run_steps(act, step, SECTIONS, 2)
            act.wait_ge(d_y, 48 * BLKS)
            act.wait_ge(d_f, 16 * (2 + 2 * NB) * BLKS)

        @block.tensor
        def _(pe):
            pe.wait_ge(zeroed, 1)

            def step(n):
                Z = zc[:, n.slot(2)]
                w = lambda a, g: Z[:, Z_W + (a * GB + g) * 128:Z_W + (a * GB + g + 1) * 128]
                m = lambda g: Z[:, Z_M + g * 128:Z_M + (g + 1) * 128]
                c = lambda g: Z[:, Z_C + g * 128:Z_C + (g + 1) * 128]
                cJ = lambda g: Z[:, Z_CJ + g * 128:Z_CJ + (g + 1) * 128]
                ident = const["ident"]
                pe.wait_ge(d_h, n.times(16 * 4 * NB) + 16 * 4 * NB)
                wait(pe, ya, n.times(GB))
                pe.wait_ge(grouped, n.times(1) + 1)
                wait(pe, hso, n.times(1))
                wait(pe, fino, n.times(1))
                for g in range(GB):
                    for h in range(HALF):
                        pe.transpose(ps_u[:, g * NCH + h * 128:g * NCH + (h + 1) * 128], ug[:, h, g].rearrange("p s c -> p (s c)"), ident[:, :])
                for g in range(GB):
                    pe.transpose(ps_y[0][:, g * NB:(g + 1) * NB], uSg[:, g].rearrange("p s c -> p (s c)"), ident[0:NB, 0:NB])
                for a in range(2):
                    mm = pe.transpose(ps_y[1][:, a * 64:(a + 1) * 64], hin[:, 2 * a:2 * a + 2, :].rearrange("p a n -> p (a n)"),
                                      ident[0:NB * GB, 0:NB * GB])
                mm.then_inc(uTp, 1)

                def v(g):
                    at = n.times(GB) + g
                    wait(pe, gmul, at - (g > 0))
                    for a in range(2):
                        mm = pe.matmul(ps_v[g % 2][:, a * NCH:(a + 1) * NCH], w(a, g), uT[:, g, :], start=True, stop=True)
                    mm.then_inc(v_ps, 1)

                def out(g):
                    at = n.times(GB) + g
                    ps = ps_y[g % 2]
                    wait(pe, ya, at - (g > 0))
                    pe.matmul(ps[0:NB, 256:256 + TS * CH], uTS[:, g, :], m(g)[:, TS * CH:], start=True, stop=False)
                    pe.matmul(ps[0:NB, 256:256 + TS * CH], h0[:, 0, g, :], c(g)[:, 0:TS * CH], start=False, stop=True)
                    pe.wait_ge(turned, at + 1)
                    for h in range(HALF):
                        o = ps[:, h * 128:(h + 1) * 128]
                        pe.matmul(o, uT[:, g, h * 128:(h + 1) * 128], m(g), start=True, stop=False)
                        pe.matmul(o, H[:, g % 2, 0, h * 128:(h + 1) * 128], c(g), start=False, stop=False)
                        mm = pe.matmul(o, H[:, g % 2, 1, h * 128:(h + 1) * 128], cJ(g), start=False, stop=True)
                    mm.then_inc(yp, 1)

                pe.wait_ge(uTa, n.times(1) + 1)
                pe.wait_ge(uTd, n.times(1) + 1)
                pe.wait_ge(uSs, n.times(1) + 1)
                pe.wait_ge(d_zc[n.slot(2)], n.times(16, 2) + 16)
                v(0)
                for g in range(GB):
                    mm = pe.matmul(ps_u[:, g * NB:(g + 1) * NB], w(0, g), uTS[:, g, :], start=True, stop=True)
                mm.then_inc(h0s, 1)
                for g in range(GB):
                    if g + 1 < GB:
                        v(g + 1)
                    out(g)
                pe.wait_ge(s_blk, n.times(1) + 1)
                pe.matmul(ps_u[0:GB, 512:640], fin[:, 0, :], ident[:, :], start=True, stop=False)
                pe.matmul(ps_u[0:GB, 512:640], fin[:, 1, :], keep["turn"][:, :], start=False, stop=True).then_inc(finp, 1)
                pe.wait_ge(hsp, n.times(1) + 1)
                pe.matmul(ps_u[0:NB * GB, 1024:1152], hl[:, :, :].rearrange("p b g -> p (b g)"), ident[:, :], start=True, stop=True).then_inc(s_pe_hs, 1)

            run_steps(pe, step, SECTIONS, 2)

        @block.vector
        def _(dve):
            def step(n):
                st = Steps(dve, s_dve, n.times(RUN_STEPS))
                tabs = zc[:, n.slot(2), Z_T:Z_COLS].rearrange("p (a g k) -> p a g k", a=2, g=GB)
                g0 = bass.ds(n.times(GB), GB)
                dve.wait_ge(uTp, n.times(1) + 1)
                wait(dve, yp, n.times(GB))
                dve.tensor_copy(uT[:, 4:8, :].rearrange("p g k -> p (g k)"), ps_u[:, 1024:2048]).then_inc(uTd, 1)
                wait(dve, s_pe_hs, n.times(1))
                dve.tensor_copy(uTS[:, :, :].rearrange("p g b -> p (g b)"), ps_y[0][:, 0:GB * NB])
                dve.tensor_copy(h0[:, 0], ps_y[1][:, 0:64].rearrange("p (b g) -> p g b", g=GB))
                dve.tensor_scalar(h0[:, 1], ps_y[1][:, 64:128].rearrange("p (b g) -> p g b", g=GB), keep["nsgn"][:, :], None, ALU.mult).then_inc(uSs, 1)
                dve.memset(gate[:, :], 0.0)
                st.did(dve.tensor_copy(rho[:, :], keep["rho8"][:, g0]))
                for a in range(2):
                    st.did(dve.tensor_copy(p4[:, a, :], keep["pw"][:, a, g0, TS]))
                st.wait()
                dve.wait_ge(uSs, n.times(1) + 1)
                pr, pi = (bc(p4[:, a, :].unsqueeze(2), [128, GB, NB]) for a in range(2))
                dve.tensor_tensor(ha[:, 0], pr, h0[:, 0], ALU.mult)
                st.link(dve.tensor_tensor(ha[:, 1], pi, h0[:, 1], ALU.mult))
                st.link(dve.tensor_tensor(ha[:, 0], ha[:, 0], ha[:, 1], ALU.add))
                dve.wait_ge(h0s, n.times(1) + 1)
                dve.tensor_tensor(hl[:, :, :].rearrange("p b g -> p g b"), ha[:, 0], ps_u[:, 0:GB * NB].rearrange("p (g b) -> p g b", b=NB), ALU.add).then_inc(hsp, 1)
                dve.wait_ge(d_zc[n.slot(2)], n.times(16, 2) + 16)
                for g in range(GB):
                    q, at = g % 2, n.times(GB) + g
                    dve.wait_ge(v_ps, at + 1)
                    dve.tensor_tensor(g1[:, q, :], ps_v[q][:, 0:NCH], tabs[:, 0, g, :], ALU.mult)
                    dve.tensor_tensor(g2[:, q, :], ps_v[q][:, NCH:], tabs[:, 1, g, :], ALU.mult).then_inc(gmul, 1)
                    dve.wait_ge(gmul, at + 1)
                    st.link(dve.tensor_tensor(g1[:, q, :], g1[:, q, :], g2[:, q, :], ALU.subtract))
                    wait(dve, turned, at - (g > 0))
                    dve.tensor_tensor_scan(G[:, q, :], bc(rho[:, g:g + 1], [128, NCH]), g1[:, q, :], 0.0, ALU.mult, ALU.add).then_inc(scanned, 1)
                dve.wait_ge(finp, n.times(1) + 1)
                wait(dve, d_f, n.times(16 * (2 + 2 * NB)))
                dve.tensor_copy(finT[:, :], ps_u[0:GB, 512:640]).then_inc(fino, 1)
                dve.wait_ge(s_pe_hs, n.times(1) + 1)
                dve.tensor_copy(hsT[:, :], ps_u[0:NB * GB, 1024:1152]).then_inc(hso, 1)
                assert st.n == RUN_STEPS, st.n

            run_steps(dve, step, SECTIONS, 2)


RUN_STEPS = 5 + GB


def sample_attention_stage(nc, t, const):
    TILES = 9
    NEW = 3 * TS
    COLS = TILES * 128 + NEW
    BANKS = ((0, 512), (512, 1024), (1024, COLS))
    R = TS * HEADS
    PAIRS = AW // 128
    GT = TILES + 1
    SCALE = HD ** -0.5
    SECTIONS = ((0, NB - 2, True), (NB - 2, NB, False))
    with ExitStack() as ctx:
        P = Pool_(nc, ctx)
        kt = P.sb("b_k", [128, 2, TILES, AW])
        vt = P.sb("b_v", [128, 2, TILES, AW])
        kn = P.sb("b_kn", [NEW, 2, AW])
        vn = P.sb("b_vn", [NEW, 2, AW])
        q = P.sb("b_q", [R, 2, AW])
        qd = P.sb("b_qd", [R, AW])
        qT = P.sb("b_qT", [128, PAIRS, R])
        kT = P.sb("b_kT", [128, PAIRS, COLS])
        mask = P.sb("b_mask", [R, COLS])
        pr = P.sb("b_pr", [R, COLS])
        prT = P.sb("b_prT", [128, TILES + 1, R])
        own = P.sb("b_own", [R, HEADS])
        sel = P.sb("b_sel", [R, 128])
        top, ntop, den, rden = (P.sb("b_" + x, [R, 1]) for x in ("top", "ntop", "den", "rden"))
        om = P.sb("b_om", [R, AW])
        out = P.sb("b_out", [TS, AW])
        ps_t = [P.ps(f"b_ps_t{x}", [128, 512]) for x in range(2)]
        ps_s = [P.ps(f"b_ps_s{x}", [128, 512]) for x in range(3)]
        ps_p = P.ps("b_ps_p", [128, 512])
        ps_o = P.ps("b_ps_o", [128, 512])
        ps_f = P.ps("b_ps_f", [128, 512])
        d_k, d_v = P.sem2("b_dk"), P.sem2("b_dv")
        (made, s_sel, kTp, kTa, kTd, qm, scored, masked, s_top, shift, exped, pTp, pTs, pvp, rd, omd, fp, fo, d_o) = (P.sem("b_" + x) for x in (
            "made", "s_sel", "kTp", "kTa", "kTd", "qm", "scored", "masked", "top_s", "shift", "exped", "pTp", "pTs", "pvp", "rd", "omd", "fp", "fo", "do"))
        block = ctx.enter_context(nc.Block())

        @block.sync
        def _(sp):
            def step(n):
                p = n.slot(2)
                for name, new, dst, dstn, sem in (("cache_k", "k_new", kt, kn, d_k), ("cache_v", "v_new", vt, vn, d_v)):
                    if sem is d_k:
                        wait(sp, kTp, n.times(GT) - GT)
                    else:
                        wait(sp, pvp, n.times(1) - 1)
                    seq = t[name][bass.ds(n.idx, 1)].squeeze(0)
                    sp.dma_start(dst[:, p, 0:TS, :], seq.rearrange("(n d) c -> n d c", d=16)[:, 0:TS, :]).then_inc(sem[p], 16)
                    sp.dma_start(dst[:, p, TS:2 * TS, :], seq[PAST - 512:, :].rearrange("(n d) c -> n d c", d=4)).then_inc(sem[p], 16)
                    sp.dma_start(dst[:, p, 2 * TS, :], seq[PAST - 128:, :]).then_inc(sem[p], 16)
                    for j in range(3):
                        sp.dma_start(dstn[j * TS:(j + 1) * TS, p, :], t[new][bass.ds(n.times(TS), TS), :]).then_inc(sem[p], 16)
                    if sem is d_k:
                        for j in range(TS):
                            sp.dma_start(q[j * HEADS:(j + 1) * HEADS, p, :],
                                         t["q"][bass.ds(n.times(TS) + (SEQ + j), 1), :].broadcast_to([HEADS, AW])).then_inc(sem[p], 16)

            step(Turn(0))
            step(Turn(1))
            run_steps(sp, step, ((2, NB, True),), 2)

        @block.gpsimd
        def _(pool):
            pool.memset(mask[:, :], 0.0).then_inc(made, 1)
            pool.wait_ge(made, 1)
            wide = mask[:, 0:2 * TS * 128].rearrange("p (a r k) -> p a r k", a=2, r=TS)
            last = mask[:, 2 * TS * 128:TILES * 128]
            new = mask[:, TILES * 128:].rearrange("p (a k) -> p a k", a=3)

            def select(view, pattern, base, mult):
                pool.affine_select(out=view, in_=view, compare_op=ALU.is_ge, fill=NEG, base=base, pattern=pattern,
                                   channel_multiplier=mult).then_inc(made, 1)

            select(wide, [[0, 2], [HEADS, TS], [0, 128]], HEADS - 1, -1)
            select(last, [[HEADS, 128]], HEADS - 1, -1)
            select(new, [[0, 3], [-HEADS, TS]], 0, 1)
            pool.wait_ge(made, 4)
            select(wide, [[0, 2], [-HEADS, TS], [0, 128]], 0, 1)
            select(new[:, 1:3, :], [[0, 2], [HEADS, TS]], HEADS - 1, -1)

        @block.tensor
        def _(pe):
            ident = const["ident"]

            def transposes(n):
                p = n.slot(2)
                pe.wait_ge(d_k[p], n.times(160, 2) + 160)
                for g in range(GT):
                    wait(pe, (kTa, kTd)[g % 2], n.times(GT // 2) + g // 2)
                    if g == TILES:
                        pe.wait_ge(qm, n.times(1) + 1)
                        for j in range(PAIRS):
                            pe.matmul(ps_t[g % 2][:, 128 + j * R:128 + (j + 1) * R], qd[:, j * 128:(j + 1) * 128],
                                      ident[0:R, 0:R], start=True, stop=True)
                    for j in range(PAIRS):
                        cols = slice(j * 128, (j + 1) * 128)
                        if g < TILES:
                            mm = pe.transpose(ps_t[g % 2][:, cols], kt[:, p, g, cols], ident[:, :])
                        else:
                            mm = pe.transpose(ps_t[g % 2][:, j * NEW:(j + 1) * NEW], kn[:, p, cols], ident[0:NEW, 0:NEW])
                    mm.then_inc(kTp, 1)

            def scores(n):
                pe.wait_ge(kTa, n.times(GT // 2) + GT // 2)
                pe.wait_ge(kTd, n.times(GT // 2) + GT // 2)
                wait(pe, masked, n.times(1))
                for b, (c0, c1) in enumerate(BANKS):
                    for j in range(PAIRS):
                        mm = pe.matmul(ps_s[b][0:R, 0:c1 - c0], qT[:, j, :], kT[:, j, c0:c1], start=(j == 0), stop=(j == PAIRS - 1))
                mm.then_inc(scored, 1)

            def values(n):
                p = n.slot(2)
                pe.wait_ge(exped, n.times(1) + 1)
                for g in range(TILES):
                    pe.matmul(ps_p[:, g * R:(g + 1) * R], pr[:, g * 128:(g + 1) * 128], ident[0:R, 0:R], start=True, stop=True)
                pe.matmul(ps_p[0:NEW, TILES * R:(TILES + 1) * R], pr[:, TILES * 128:COLS], ident[0:R, 0:R],
                          start=True, stop=True).then_inc(pTp, 1)
                pe.wait_ge(d_v[p], n.times(96, 2) + 96)
                pe.wait_ge(pTs, n.times(1) + 1)
                wait(pe, omd, n.times(1))
                for g in range(TILES):
                    pe.matmul(ps_o[0:R, :], prT[:, g, :], vt[:, p, g, :], start=(g == 0), stop=False)
                pe.matmul(ps_o[0:R, :], prT[0:NEW, TILES, :], vn[:, p, :], start=False, stop=True).then_inc(pvp, 1)

            def step(n):
                last = n.i is None and n.add == NB - 1
                if not last:
                    transposes(n + 1)
                values(n)
                if not last:
                    scores(n + 1)
                pe.wait_ge(omd, n.times(1) + 1)
                pe.matmul(ps_f[:, :], sel[:, :], om[:, :], start=True, stop=True).then_inc(fp, 1)

            transposes(Turn(0))
            scores(Turn(0))
            run_steps(pe, step, SECTIONS, 2)

        @block.scalar
        def _(act):
            def keys_out(n):
                wait(act, scored, n.times(1))
                for g in range(0, GT, 2):
                    act.wait_ge(kTp, n.times(GT) + g + 1)
                    act.activation(kT[:, :, g * 128:(g + 1) * 128], ps_t[0][:, :].rearrange("p (j k) -> p j k", j=PAIRS), ACT.Copy).then_inc(kTa, 1)

            def step(n):
                act.wait_ge(shift, n.times(1) + 1)
                wait(act, rd, n.times(1))
                act.activation(pr[:, :], pr[:, :], ACT.Exp, scale=SCALE, bias=ntop[:, :], accum_out=den[:, :]).then_inc(exped, 1)
                if n.i is not None or n.add < NB - 1:
                    keys_out(n + 1)
                act.wait_ge(fo, n.times(1) + 1)
                act.dma_start(t["att_new"][bass.ds(n.times(TS), TS), :], out[:, :]).then_inc(d_o, 16)

            keys_out(Turn(0))
            run_steps(act, step, SECTIONS, 2)
            act.wait_ge(d_o, 16 * NB)

        @block.vector
        def _(dve):
            i32 = const["ident"][0:R, 0:R]
            dve.tensor_reduce(own[:, :], i32.rearrange("p (t h) -> p h t", t=TS), AX.X, ALU.add)
            dve.memset(sel[:, :], 0.0).then_inc(s_sel, 1)
            dve.wait_ge(s_sel, 1)
            dve.tensor_reduce(sel[:, 0:TS], i32.rearrange("p (t h) -> p t h", t=TS), AX.X, ALU.add).then_inc(s_sel, 1)
            dve.wait_ge(s_sel, 2)
            dve.wait_ge(made, 6)
            own3 = bc(own[:, :].unsqueeze(2), [R, HEADS, HD])

            def keys_out(n):
                p = n.slot(2)
                dve.wait_ge(d_k[p], n.times(160, 2) + 160)
                wait(dve, kTp, n.times(GT))
                dve.tensor_tensor(qd[:, :].rearrange("p (h d) -> p h d", h=HEADS), q[:, p].rearrange("p (h d) -> p h d", h=HEADS),
                                  own3, ALU.mult).then_inc(qm, 1)
                wait(dve, scored, n.times(1))
                for g in range(1, GT, 2):
                    dve.wait_ge(kTp, n.times(GT) + g + 1)
                    if g < TILES:
                        dve.tensor_copy(kT[:, :, g * 128:(g + 1) * 128], ps_t[1][:, :].rearrange("p (j k) -> p j k", j=PAIRS)).then_inc(kTd, 1)
                    else:
                        dve.tensor_copy(kT[:, :, g * 128:], ps_t[1][:, 0:PAIRS * NEW].rearrange("p (j k) -> p j k", j=PAIRS))
                        dve.tensor_copy(qT[:, :, :].rearrange("p j r -> p (j r)"), ps_t[1][:, 128:128 + PAIRS * R]).then_inc(kTd, 1)

            def step(n):
                dve.wait_ge(scored, n.times(1) + 1)
                for b, (c0, c1) in enumerate(BANKS):
                    add = dve.tensor_tensor(pr[:, c0:c1], ps_s[b][0:R, 0:c1 - c0], mask[:, c0:c1], ALU.add)
                add.then_inc(masked, 1)
                dve.wait_ge(masked, n.times(1) + 1)
                dve.tensor_reduce(top[:, :], pr[:, :], AX.X, ALU.max).then_inc(s_top, 1)
                dve.wait_ge(s_top, n.times(1) + 1)
                dve.tensor_scalar(ntop[:, :], top[:, :], -SCALE, None, ALU.mult).then_inc(shift, 1)
                if n.i is not None or n.add < NB - 1:
                    keys_out(n + 1)
                dve.wait_ge(pTp, n.times(1) + 1)
                dve.tensor_copy(prT[:, 0:TILES, :].rearrange("p g r -> p (g r)"), ps_p[:, 0:TILES * R])
                dve.tensor_copy(prT[0:NEW, TILES, :], ps_p[0:NEW, TILES * R:(TILES + 1) * R]).then_inc(pTs, 1)
                dve.reciprocal(rden[:, :], den[:, :]).then_inc(rd, 1)
                dve.wait_ge(rd, n.times(1) + 1)
                dve.wait_ge(pvp, n.times(1) + 1)
                wait(dve, fp, n.times(1))
                dve.scalar_tensor_tensor(om[:, :].rearrange("p (h d) -> p h d", h=HEADS), ps_o[0:R, :].rearrange("p (h d) -> p h d", h=HEADS),
                                         rden[:, :], own3, ALU.mult, ALU.mult).then_inc(omd, 1)
                wait(dve, d_o, n.times(16))
                dve.wait_ge(fp, n.times(1) + 1)
                dve.tensor_copy(out[:, :], ps_f[0:TS, :]).then_inc(fo, 1)

            keys_out(Turn(0))
            run_steps(dve, step, SECTIONS, 2)


def mix_stage(nc, t, const):
    TILES = SEQ // 128 + 1
    SECTIONS = ((0, 1, False), (1, TILES - 4, True), (TILES - 4, TILES, False))
    KS = SW // 128
    NP = len(DILATIONS)
    with ExitStack() as ctx:
        P = Pool_(nc, ctx)
        w_out = P.sb("c_wout", [128, KT, D])
        w_glu = P.sb("c_wglu", [128, KS, SW])
        gain = P.sb("c_gain", [128, KT])
        g2 = P.sb("c_g2", [128, D])
        gate1 = P.sb("c_gate1", [128, 2, D])
        A2 = P.sb("c_A2", [128, 2, D])
        B2 = P.sb("c_B2", [128, 2, D])
        ot = P.sb("c_ot", [128, 2, NP, OROW])
        y = P.sb("c_y", [128, 2, SW])
        x = P.sb("c_x", [128, 2, D])
        big = P.sb("c_big", [128, HEADS])
        wt = P.sb("c_wt", [128, NP, HEADS])
        wd = P.sb("c_wd", [128, NP, HEADS])
        oa = P.sb("c_oa", [128, AW])
        yT = P.sb("c_yT", [128, KS, 128])
        sg = P.sb("c_sg", [128, SW])
        ym = P.sb("c_ym", [128, SW])
        ss = P.sb("c_ss", [128, 3, 2])
        junk = P.sb("c_junk", [128, D])
        m = P.sb("c_m", [128, D])
        mT = P.sb("c_mT", [128, KT, 128])
        x1 = P.sb("c_x1", [128, 2, D])
        s2 = P.sb("c_s2", [128, 3])
        h2 = P.sb("c_h2", [128, D])
        h2T = P.sb("c_h2T", [128, KT, 128])
        ps_yT = P.ps("c_ps_yT", [128, 512])
        ps_glu = P.ps("c_ps_glu", [128, 512])
        ps_mT = P.ps("c_ps_mT", [128, D])
        ps_w = P.ps("c_ps_w", [128, D])
        ps_h = P.ps("c_ps_h", [128, D])
        d_w, d_g = P.sem("c_dw"), P.sem("c_dg")
        d_a, d_x, d_1, d_h = P.sem2("c_da"), P.sem2("c_dx"), P.sem2("c_d1"), const["h2_stored"]
        (ready, yTp, yTs, gap, expd, merged, oasq, glu, sig, ymd, roots, recips, md, mTp, mTa, mTd, wo, x1d, x1sq, r2, h2d, hTp, hTa, hTd,
         s_dve, s_mul, s_rec, s_fold) = (P.sem("c_" + v) for v in ("ready", "yTp", "yTs", "gap", "expd", "merged", "oasq", "glu_s", "sig", "ymd", "roots",
             "recips", "md", "mTp", "mTa", "mTd", "wo", "x1d", "x1sq", "r2", "h2d", "hTp", "hTa", "hTd", "s_dve", "s_mul", "s_rec", "s_fold"))
        block = ctx.enter_context(nc.Block())

        def wait_store(eng, n):
            p = n.slot(2)
            wait(eng, d_h[1 - p], n.times(16, 2) + (16 if p else 0))

        def exists(n):
            return n.i is not None or 0 <= n.add < TILES

        @block.sync
        def _(sp):
            def load_a(n):
                p, r = n.slot(2), rows_of(n)
                if is_sample(n):
                    sp.dma_start(ot[0:r, p, 0, 0:AW], t["att_new"]).then_inc(d_a[p], 16)
                else:
                    sp.dma_start(ot[:, p], t["o"].rearrange("a n c -> n a c")[tile_rows(n)]).then_inc(d_a[p], 16)
                sp.dma_start(y[0:r, p], t["y"][tile_rows(n), :]).then_inc(d_a[p], 16)

            def load_x(n):
                p, r = n.slot(2), rows_of(n)
                sp.dma_start(x[0:r, p], t["x_sample"] if is_sample(n) else t["x_prompt"][tile_rows(n), :]).then_inc(d_x[p], 16)

            load_a(Turn(0))
            sp.dma_start(w_glu[:, :, :], t["w_glu"].rearrange("(k p) n -> p k n", p=128)).then_inc(d_w, 16)
            sp.dma_start(w_out[:, :, :], t["w_out"].rearrange("(k p) n -> p k n", p=128)).then_inc(d_g, 16)
            for k in range(KT):
                name, at = ("attn_out_g", k) if k < AW // 128 else ("ssm_out_g", k - AW // 128)
                sp.dma_start(gain[:, k:k + 1], t[name].rearrange("(n o) -> n o", o=1)[at * 128:(at + 1) * 128, :]).then_inc(d_g, 16)
            sp.dma_start(g2[:, :], t["norm2_g"].rearrange("(o n) -> o n", o=1).broadcast_to([128, D])).then_inc(d_g, 16)
            for which, dst in ((2, gate1), (3, B2), (4, A2)):
                load_modulation(sp, t, dst[:, 0], which, d_g, False)
                load_modulation(sp, t, dst[0:NS, 1], which, d_g, True)
            load_x(Turn(0))
            load_a(Turn(1))
            load_x(Turn(1))
            sp.wait_ge(ymd, 1)
            sp.wait_ge(merged, 1)
            load_a(Turn(2))

            def step(n):
                p, r = n.slot(2), rows_of(n)
                if exists(n + 3):
                    sp.wait_ge(ymd, n.times(1) + 2)
                    sp.wait_ge(merged, n.times(1) + 2)
                    load_a(n + 3)
                sp.wait_ge(x1d, n.times(1) + 1)
                if exists(n + 2):
                    load_x(n + 2)
                sp.dma_start(t["x1"][tile_rows(n), :], x1[0:r, p]).then_inc(d_1[p], 16)

            run_steps(sp, step, SECTIONS, 2)
            for p in range(2):
                sp.wait_ge(d_1[p], 16 * ((TILES + 1 - p) // 2))

        @block.gpsimd
        def _(pool):
            def store_h(n):
                r = rows_of(n)
                pool.wait_ge(hTa, n.times(1) + 1)
                pool.wait_ge(hTd, n.times(1) + 1)
                cols = tile_rows(n)
                pool.dma_start(t["h2T"][:, :, cols], h2T[:, :, 0:r]).then_inc(d_h[n.slot(2)], 16)

            def step(n):
                r, j = rows_of(n), 1 if is_sample(n) else 0
                pool.wait_ge(s_dve, n.times(1) + 1)
                pool.tensor_tensor(h2[0:r, :], h2[0:r, :], B2[0:r, j], ALU.add).then_inc(h2d, 1)
                if n.i is not None or n.add > 0:
                    store_h(n + -1)

            run_steps(pool, step, SECTIONS, 2)
            store_h(Turn(TILES - 1))
            for p in range(2):
                pool.wait_ge(d_h[p], 16 * ((TILES + 1 - p) // 2))

        @block.tensor
        def _(pe):
            ident = const["ident"]

            def gates(n):
                r, p = rows_of(n), n.slot(2)
                pe.wait_ge(d_a[p], n.times(32, 2) + 32)
                for k in range(KS):
                    mm = pe.transpose(ps_yT[:, k * 128:k * 128 + r], y[0:r, p, k * 128:(k + 1) * 128], ident[0:r, 0:r])
                mm.then_inc(yTp, 1)
                if n.i is None and n.add == 0:
                    pe.wait_ge(d_w, 16)
                wait(pe, sig, n.times(1))
                pe.wait_ge(yTs, n.times(1) + 1)
                for k in range(KS):
                    mm = pe.matmul(ps_glu[0:r, :], yT[:, k, 0:r], w_glu[:, k, :], start=(k == 0), stop=(k == KS - 1))
                mm.then_inc(glu, 1)

            def merged_T(n):
                r = rows_of(n)
                wait(pe, mTa, n.times(1))
                wait(pe, mTd, n.times(1))
                pe.wait_ge(md, n.times(2) + 2)
                for k in range(KT):
                    mm = pe.transpose(ps_mT[:, k * 128:k * 128 + r], m[0:r, k * 128:(k + 1) * 128], ident[0:r, 0:r])
                mm.then_inc(mTp, 1)

            def project(n):
                r = rows_of(n)
                pe.wait_ge(mTa, n.times(1) + 1)
                wait(pe, x1d, n.times(1))
                pe.wait_ge(mTd, n.times(1) + 1)
                for c in range(2):
                    for k in range(KT):
                        mm = pe.matmul(ps_w[0:r, c * 512:(c + 1) * 512], mT[:, k, 0:r], w_out[:, k, c * 512:(c + 1) * 512],
                                       start=(k == 0), stop=(k == KT - 1))
                mm.then_inc(wo, 1)

            def normed_T(n):
                r = rows_of(n)
                wait(pe, hTa, n.times(1))
                wait(pe, hTd, n.times(1))
                pe.wait_ge(h2d, n.times(1) + 1)
                for k in range(KT):
                    mm = pe.transpose(ps_h[:, k * 128:k * 128 + r], h2[0:r, k * 128:(k + 1) * 128], ident[0:r, 0:r])
                mm.then_inc(hTp, 1)

            def step(n):
                last = n.i is None and n.add == TILES - 1
                if not last:
                    gates(n + 1)
                project(n)
                if n.i is not None or n.add > 0:
                    normed_T(n + -1)
                if not last:
                    merged_T(n + 1)

            gates(Turn(0))
            merged_T(Turn(0))
            pe.wait_ge(ready, 1)
            run_steps(pe, step, SECTIONS, 2)
            normed_T(Turn(TILES - 1))

        @block.scalar
        def _(act):
            def ahead(n):
                r, p = rows_of(n), n.slot(2)
                act.wait_ge(yTp, n.times(1) + 1)
                wait(act, glu, n.times(1))
                act.activation(yT[:, :, 0:r], ps_yT[:, :].rearrange("p (k n) -> p k n", n=128)[:, :, 0:r], ACT.Copy).then_inc(yTs, 1)
                if not is_sample(n):
                    act.wait_ge(gap, n.times(1) + 1)
                    act.activation(wt[0:r], wt[0:r], ACT.Exp, scale=HD ** -0.5).then_inc(expd, 1)
                act.wait_ge(merged, n.times(1) + 1)
                wait(act, recips, n.times(1))
                act.activation(junk[0:r, 0:AW], oa[0:r, :], ACT.Square, accum_out=ss[0:r, 0, 0:1]).then_inc(oasq, 1)
                act.wait_ge(glu, n.times(1) + 1)
                wait(act, ymd, n.times(1))
                act.activation(sg[0:r, :], ps_glu[0:r, :], ACT.Sigmoid).then_inc(sig, 1)
                act.wait_ge(ymd, n.times(1) + 1)
                act.wait_ge(oasq, n.times(2) + 1)
                act.activation(junk[0:r, 0:SW], ym[0:r, :], ACT.Square, accum_out=ss[0:r, 0, 1:2]).then_inc(oasq, 1)
                act.wait_ge(oasq, n.times(2) + 2)
                wait(act, recips, n.times(1))
                act.activation(ss[0:r, 1, :], ss[0:r, 0, :], ACT.Sqrt, scale=1.0 / AW, bias=const["eps"][0:r, :]).then_inc(roots, 1)
                wait(act, mTp, n.times(1))
                act.wait_ge(recips, n.times(1) + 1)
                act.activation(m[0:r, 0:AW], oa[0:r, :], ACT.Copy, scale=ss[0:r, 2, 0:1]).then_inc(md, 1)
                act.activation(m[0:r, AW:], ym[0:r, :], ACT.Copy, scale=ss[0:r, 2, 1:2]).then_inc(md, 1)

            def halves(n):
                r = rows_of(n)
                act.wait_ge(hTp, n.times(1) + 1)
                wait_store(act, n)
                act.activation(h2T[:, 0:4, 0:r], ps_h[:, 0:512].rearrange("p (k n) -> p k n", n=128)[:, :, 0:r], ACT.Copy).then_inc(hTa, 1)

            def mT_out(n):
                r = rows_of(n)
                wait(act, wo, n.times(1))
                act.wait_ge(mTp, n.times(1) + 1)
                act.activation(mT[:, 0:4, 0:r], ps_mT[:, 0:512].rearrange("p (k n) -> p k n", n=128)[:, :, 0:r], ACT.Copy).then_inc(mTa, 1)

            def step(n):
                r, p = rows_of(n), n.slot(2)
                last = n.i is None and n.add == TILES - 1
                if not last:
                    ahead(n + 1)
                if n.i is not None or n.add > 0:
                    halves(n + -1)
                if not last:
                    mT_out(n + 1)
                act.wait_ge(x1d, n.times(1) + 1)
                act.wait_ge(oasq, (n.times(2) + 4) if not last else 2 * TILES)
                act.activation(junk[0:r, :], x1[0:r, p], ACT.Square, accum_out=s2[0:r, 0:1]).then_inc(x1sq, 1)
                act.wait_ge(x1sq, n.times(1) + 1)
                act.activation(s2[0:r, 1:2], s2[0:r, 0:1], ACT.Sqrt, scale=1.0 / D, bias=const["eps"][0:r, :]).then_inc(r2, 1)

            ahead(Turn(0))
            mT_out(Turn(0))
            run_steps(act, step, SECTIONS, 2)
            halves(Turn(TILES - 1))

        @block.vector
        def _(dve):
            dve.wait_ge(d_g, 16 * (KT + 8))
            for k in range(KT):
                dve.tensor_scalar(w_out[:, k], w_out[:, k], gain[:, k:k + 1], None, ALU.mult)
            for j, r in ((0, 128), (1, NS)):
                last = dve.scalar_tensor_tensor(A2[0:r, j], A2[0:r, j], 1.0, g2[0:r, :], ALU.add, ALU.mult)
            last.then_inc(ready, 1)
            dve.wait_ge(ready, 1)

            def fold(n):
                return Steps(dve, s_fold, n.times(FOLD))

            def ahead(n):
                r, p = rows_of(n), n.slot(2)
                st = fold(n)
                dve.wait_ge(d_a[p], n.times(32, 2) + 32)
                wait(dve, md, n.times(2))
                o3 = oa[0:r, :].rearrange("p (h d) -> p h d", h=HEADS)
                if is_sample(n):
                    dve.tensor_copy(oa[0:r, :], ot[0:r, p, 0, 0:AW]).then_inc(merged, 1)
                else:
                    mx = ot[:, p, :, AW:AW + HEADS]
                    st.link(dve.tensor_tensor(big[:, :], mx[:, 0], mx[:, 1], ALU.max))
                    st.link(dve.tensor_tensor(big[:, :], big[:, :], mx[:, 2], ALU.max))
                    dve.tensor_tensor(wt[:, :, :], mx, bc(big[:, :].unsqueeze(1), [128, NP, HEADS]), ALU.subtract).then_inc(gap, 1)
                    dve.wait_ge(expd, n.times(1) + 1)
                    st.link(dve.tensor_tensor(wd[:, :, :], wt[:, :, :], ot[:, p, :, AW + HEADS:], ALU.mult))
                    st.link(dve.tensor_tensor(big[:, :], wd[:, 0], wd[:, 1], ALU.add))
                    st.link(dve.tensor_tensor(big[:, :], big[:, :], wd[:, 2], ALU.add))
                    st.link(dve.reciprocal(big[:, :], big[:, :]))
                    st.link(dve.tensor_tensor(wt[:, :, :], wt[:, :, :], bc(big[:, :].unsqueeze(1), [128, NP, HEADS]), ALU.mult))
                    part = [ot[:, p, a, 0:AW].rearrange("p (h d) -> p h d", h=HEADS) for a in range(NP)]
                    for a in range(NP):
                        st.did(dve.tensor_tensor(part[a], part[a], bc(wt[:, a, :].unsqueeze(2), [128, HEADS, HD]), ALU.mult))
                    st.wait()
                    st.link(dve.tensor_tensor(o3, part[0], part[1], ALU.add))
                    dve.tensor_tensor(o3, o3, part[2], ALU.add).then_inc(merged, 1)
                    assert st.n == FOLD
                dve.wait_ge(sig, n.times(1) + 1)
                dve.tensor_tensor(ym[0:r, :], y[0:r, p], sg[0:r, :], ALU.mult).then_inc(ymd, 1)
                dve.wait_ge(roots, n.times(1) + 1)
                dve.reciprocal(ss[0:r, 2, :], ss[0:r, 1, :]).then_inc(recips, 1)

            def halves(n):
                r = rows_of(n)
                dve.wait_ge(hTp, n.times(1) + 1)
                wait_store(dve, n)
                dve.tensor_copy(h2T[:, 4:8, 0:r], ps_h[:, 512:].rearrange("p (k n) -> p k n", n=128)[:, :, 0:r]).then_inc(hTd, 1)

            def mT_out(n):
                r = rows_of(n)
                wait(dve, wo, n.times(1))
                dve.wait_ge(mTp, n.times(1) + 1)
                dve.tensor_copy(mT[:, 4:8, 0:r], ps_mT[:, 512:].rearrange("p (k n) -> p k n", n=128)[:, :, 0:r]).then_inc(mTd, 1)

            def step(n):
                r, p, j = rows_of(n), n.slot(2), 1 if is_sample(n) else 0
                last = n.i is None and n.add == TILES - 1
                if not last:
                    ahead(n + 1)
                dve.wait_ge(wo, n.times(1) + 1)
                wait(dve, d_1[p], n.times(16, 2))
                dve.tensor_tensor(x1[0:r, p], ps_w[0:r, :], gate1[0:r, j], ALU.mult).then_inc(s_mul, 1)
                dve.wait_ge(d_x[p], n.times(16, 2) + 16)
                dve.wait_ge(s_mul, n.times(1) + 1)
                dve.tensor_tensor(x1[0:r, p], x1[0:r, p], x[0:r, p], ALU.add).then_inc(x1d, 1)
                if n.i is not None or n.add > 0:
                    halves(n + -1)
                if not last:
                    mT_out(n + 1)
                dve.wait_ge(r2, n.times(1) + 1)
                dve.reciprocal(s2[0:r, 2:3], s2[0:r, 1:2]).then_inc(s_rec, 1)
                dve.wait_ge(s_rec, n.times(1) + 1)
                wait(dve, hTp, n.times(1))
                dve.scalar_tensor_tensor(h2[0:r, :], x1[0:r, p], s2[0:r, 2:3], A2[0:r, j], ALU.mult, ALU.mult).then_inc(s_dve, 1)

            ahead(Turn(0))
            mT_out(Turn(0))
            run_steps(dve, step, SECTIONS, 2)
            halves(Turn(TILES - 1))


FOLD = 11


def ffn_block(nc, t, const, a, e, cuts, window):
    HC = FF // 128
    W = e - a
    FULL = W // 128
    TILES = [(j, 128) for j in range(FULL)] + ([(FULL, NS)] if W % 128 else [])
    TURNED = [TILES[g:g + 4] for g in range(0, len(TILES), 4)]
    C, G = len(cuts), len(TURNED)
    DOWN = ((0, 2, False), (2, KT - 2, True), (KT - 2, KT, False))
    UP = ((0, 2, False), (2, HC - 2, True), (HC - 2, HC, False))
    with ExitStack() as ctx:
        P = Pool_(nc, ctx, f"_{a}")
        h2T = P.sb("f_h2T", [128, KT, W])
        aT = P.sb("f_aT", [128, HC, W])
        w = P.sb("f_w", [128, 2, 2, KT, 128])
        h2s = P.sb("f_h2s", [128, 2, KT, W], F32R)
        ws = P.sb("f_ws", [128, 2, 2, 2, KT, 128], F32R)
        wd = P.sb("f_wd", [128, 2, HC, 128])
        gate2 = P.sb("f_gate2", [128, 2, D])
        sl = P.sb("f_sl", [128, 2, 512])
        dT = P.sb("f_dT", [128, W])
        xb = P.sb("f_x1", [128, 2, len(TILES), 128])
        yb = P.sb("f_y", [128, 2, len(TILES), 128])
        ps = [[P.ps(f"f_ps{p}{x}", [128, 512]) for x in range(C)] for p in range(2)]
        ps_t = [P.ps(f"f_ps_t{x}", [128, 512]) for x in range(2)]
        d_h, d_g = P.sem("f_dh"), P.sem("f_dg")
        d_w, d_wd, d_x, d_y = P.sem2("f_dw"), P.sem2("f_dwd"), P.sem2("f_dx"), P.sem2("f_dy")
        gated, upped, silued, hidden, down, down_out, turned, scaled, y_done = (
            P.sem("f_" + v) for v in ("gated", "upped", "silued", "hidden", "down", "down_out", "turned", "scaled", "y_done"))
        h_hi, h_lo, w_hi, w_lo = (P.sem("f_" + v) for v in ("h_hi", "h_lo", "w_hi", "w_lo"))
        d_m = const["windows_moved"]
        block = ctx.enter_context(nc.Block())
        XN = 16 * (2 if len(TILES) > FULL else 1)

        def piece(arr, p, arr_t, cols):
            yield arr[:, p, 0:FULL], arr_t[0].rearrange("(j p) n -> p j n", p=128)[:, :, cols]
            if len(TILES) > FULL:
                yield arr[0:NS, p, FULL], arr_t[1][:, cols]

        @block.sync
        def _(sp):
            sp.dma_start(h2T[:, :, :], t["h2T"][:, :, a:e]).then_inc(d_h, 16)

            def load_w(n):
                p = n.slot(2)
                wait(sp, w_lo, n.times(1) - 1)
                cols = bass.ds(n.times(128), 128)
                for j, name in enumerate(("w_gate", "w_up")):
                    sp.dma_start(w[:, p, j], t[name].rearrange("(k p) n -> p k n", p=128)[:, :, cols]).then_inc(d_w[p], 16)

            def load_d(n):
                p = n.slot(2)
                cols = bass.ds(n.times(128), 128)
                wait(sp, down, n.times(C) - C)
                sp.dma_start(wd[:, p], t["w_down"].rearrange("(k p) n -> p k n", p=128)[:, :, cols]).then_inc(d_wd[p], 16)
                wait(sp, y_done, n.times(1) - 1)
                for dst, src in piece(xb, p, (t["x1"][a:a + FULL * 128, :], t["x1"][a + FULL * 128:e, :]), cols):
                    sp.dma_start(dst, src).then_inc(d_x[p], 16)

            load_w(Turn(0))
            load_w(Turn(1))
            for j in range(2):
                load_modulation(sp, t, gate2[0:(128, NS)[j], j], 5, d_g, j == 1)
            load_d(Turn(0))
            load_d(Turn(1))
            run_steps(sp, load_w, ((2, HC, True),), 2)
            run_steps(sp, load_d, ((2, KT, True),), 2)

        @block.gpsimd
        def _(pool):
            cache, new, out = (t[x] for x in window[:3])
            for b in range(*window[3:5]):
                pool.wait_ge(hidden, (4 * (b - window[3]) + 1) * C)
                pool.dma_start(out[b, 0:PAST - TS, :], cache[b, TS:PAST, :]).then_inc(d_m, 16)
                pool.dma_start(out[b, PAST - TS:PAST, :], new[b * TS:(b + 1) * TS, :]).then_inc(d_m, 16)
            pool.wait_ge(d_m, window[5])

        @block.tensor
        def _(pe):
            pe.wait_ge(h_lo, 1)

            def up(n):
                p = n.slot(2)
                pe.wait_ge(w_lo, n.times(1) + 1)
                for c, (c0, c1) in enumerate(cuts):
                    wait(pe, hidden, n.times(C) - C + c + 1)
                    for j, sem in enumerate((gated, upped)):
                        parts = [(k, a, b) for k in range(KT) for a, b in ((0, 0), (0, 1), (1, 0))]
                        for k, a, b in parts:
                            mm = pe.matmul(ps[j][c][:, 0:c1 - c0], ws[:, p, a, j, k, :], h2s[:, b, k, c0:c1],
                                           start=((k, a, b) == parts[0]), stop=((k, a, b) == parts[-1]))
                        mm.then_inc(sem, 1)

            def product(n):
                p = n.slot(2)
                pe.wait_ge(d_wd[p], n.times(16, 2) + 16)
                for c, (c0, c1) in enumerate(cuts):
                    wait(pe, down_out, n.times(C) - 2 * C + c + 1)
                    for k in range(HC):
                        mm = pe.matmul(ps[p][c][:, 0:c1 - c0], wd[:, p, k, :], aT[:, k, c0:c1], start=(k == 0), stop=(k == HC - 1))
                    mm.then_inc(down, 1)

            def turn_back(n):
                pe.wait_ge(down_out, n.times(C) + C)
                for g, tiles in enumerate(TURNED):
                    before = g - 1 if g > 1 else max(x for x in range(G) if x % 2 == g) + 1 - G
                    wait(pe, scaled, n.times(G) + before)
                    for j, r in tiles:
                        mm = pe.transpose(ps_t[g % 2][0:r, (j % 4) * 128:(j % 4 + 1) * 128], dT[:, j * 128:j * 128 + r], const["ident"][:, :])
                    mm.then_inc(turned, 1)

            run_steps(pe, up, ((0, 2, False), (2, HC, True)), 2)
            pe.wait_ge(hidden, HC * C)
            product(Turn(0))

            def step(n):
                if n.i is not None or n.add < KT - 1:
                    product(n + 1)
                turn_back(n)

            run_steps(pe, step, DOWN, 2)

        @block.scalar
        def _(act):
            def silu(n):
                for c, (c0, c1) in enumerate(cuts):
                    q = (n.add * C + c) % 2
                    act.wait_ge(gated, n.times(C) + c + 1)
                    wait(act, hidden, n.times(C) + c - 1)
                    act.activation(sl[:, q, 0:c1 - c0], ps[0][c][:, 0:c1 - c0], ACT.Silu).then_inc(silued, 1)

            def out(n):
                for c, (c0, c1) in enumerate(cuts):
                    act.wait_ge(down, n.times(C) + c + 1)
                    wait(act, turned, n.times(G))
                    act.activation(dT[:, c0:c1], ps[n.slot(2)][c][:, 0:c1 - c0], ACT.Copy).then_inc(down_out, 1)

            def store(n):
                p = n.slot(2)
                act.wait_ge(y_done, n.times(1) + 1)
                for src, dst in piece(yb, p, (t["y_prompt"][a:a + FULL * 128, :], t["y_sample"]), bass.ds(n.times(128), 128)):
                    act.dma_start(dst, src).then_inc(d_y[p], 16)

            def rounded(n):
                p = n.slot(2)
                act.wait_ge(d_w[p], n.times(32, 2) + 32)
                wait(act, upped, n.times(C) - C)
                act.activation(ws[:, p, 0], w[:, p], ACT.Copy).then_inc(w_hi, 1)

            def up_step(n):
                if n.i is not None or n.add < HC - 1:
                    rounded(n + 1)
                silu(n)

            act.wait_ge(d_h, 16)
            act.activation(h2s[:, 0], h2T[:, :, :], ACT.Copy).then_inc(h_hi, 1)
            rounded(Turn(0))
            run_steps(act, up_step, UP, 2)
            out(Turn(0))

            def step(n):
                if n.i is not None or n.add < KT - 1:
                    out(n + 1)
                store(n)

            run_steps(act, step, DOWN, 2)
            for p in range(2):
                act.wait_ge(d_y[p], XN * KT // 2)

        @block.vector
        def _(dve):
            def hide(n):
                for c, (c0, c1) in enumerate(cuts):
                    q = (n.add * C + c) % 2
                    dve.wait_ge(silued, n.times(C) + c + 1)
                    dve.wait_ge(upped, n.times(C) + c + 1)
                    dve.tensor_tensor(aT[:, hidden_row(n), c0:c1].rearrange("p o n -> p (o n)"), sl[:, q, 0:c1 - c0], ps[1][c][:, 0:c1 - c0], ALU.mult).then_inc(hidden, 1)

            def hidden_row(n):
                return bass.ds(n.idx, 1)

            def residual(n):
                p = n.slot(2)
                cols = bass.ds(n.times(128), 128)
                wait(dve, d_y[p], n.times(XN, 2))
                for g, tiles in enumerate(TURNED):
                    dve.wait_ge(turned, n.times(G) + g + 1)
                    j0, m = tiles[0][0], sum(r == 128 for _, r in tiles)
                    if m:
                        last = dve.tensor_tensor(yb[:, p, j0:j0 + m, :], ps_t[g % 2][:, 0:m * 128].rearrange("p (j n) -> p j n", n=128),
                                                 bc(gate2[:, 0, cols].unsqueeze(1), [128, m, 128]), ALU.mult)
                    if m < len(tiles):
                        last = dve.tensor_tensor(yb[0:NS, p, j0 + m, :], ps_t[g % 2][0:NS, m * 128:(m + 1) * 128], gate2[0:NS, 1, cols], ALU.mult)
                    last.then_inc(scaled, 1)
                dve.wait_ge(d_x[p], n.times(XN, 2) + XN)
                dve.wait_ge(scaled, n.times(G) + G)
                if len(TILES) > FULL:
                    dve.tensor_tensor(yb[0:NS, p, FULL], yb[0:NS, p, FULL], xb[0:NS, p, FULL], ALU.add)
                dve.tensor_tensor(yb[:, p, 0:FULL], yb[:, p, 0:FULL], xb[:, p, 0:FULL], ALU.add).then_inc(y_done, 1)

            def rest(n):
                p = n.slot(2)
                dve.wait_ge(w_hi, n.times(1) + 1)
                dve.tensor_tensor(ws[:, p, 1], w[:, p], ws[:, p, 0].bitcast(F32), ALU.subtract).then_inc(w_lo, 1)

            def up_step(n):
                if n.i is not None or n.add < HC - 1:
                    rest(n + 1)
                hide(n)

            dve.wait_ge(h_hi, 1)
            dve.tensor_tensor(h2s[:, 1], h2T[:, :, :], h2s[:, 0].bitcast(F32), ALU.subtract).then_inc(h_lo, 1)
            rest(Turn(0))
            run_steps(dve, up_step, UP, 2)
            dve.wait_ge(d_g, 32)
            run_steps(dve, residual, ((0, KT, True),), 2)


def ffn_stage(nc, t, const):
    keys, values = ("cache_k", "k_new", "k_sample"), ("cache_v", "v_new", "v_sample")
    half = NB // 2
    ffn_block(nc, t, const, 0, 512, ((0, 512),), keys + (0, half, 16 * NB))
    ffn_block(nc, t, const, 512, 1024, ((0, 512),), keys + (half, NB, 32 * NB))
    ffn_block(nc, t, const, 1024, 1536, ((0, 512),), values + (0, half, 48 * NB))
    ffn_block(nc, t, const, 1536, ROWS, ((0, 272), (272, 544)), values + (half, NB, 64 * NB))


def constants(nc, P):
    ident = P.sb("ident", [128, 128])
    eps = P.sb("eps", [128, 1])
    sgn = P.sb("sgn", [128, 1])
    nsgn = P.sb("nsgn", [128, 1])
    turn = P.sb("turn", [128, 128])
    s_ident = P.sem("s_ident")
    block_ctx = nc.Block()
    with block_ctx as block:
        @block.gpsimd
        def _(pool):
            pool.memset(ident[:, :], 0.0).then_inc(s_ident, 1)
            pool.wait_ge(s_ident, 1)
            pool.affine_select(out=ident[:, :], in_=ident[:, :], compare_op=ALU.not_equal, fill=1.0,
                               base=0, pattern=[[-1, 128]], channel_multiplier=1).then_inc(s_ident, 1)
            pool.memset(eps[:, :], EPS).then_inc(s_ident, 1)
            pool.memset(sgn[:, :], 1.0)
            pool.memset(nsgn[:, :], -1.0)
            pool.memset(turn[:, :], 0.0).then_inc(s_ident, 1)
            pool.wait_ge(s_ident, 4)
            for v, below in ((sgn, -1.0), (nsgn, 1.0)):
                pool.affine_select(out=v[:, :], in_=v[:, :], compare_op=ALU.is_ge, fill=below, base=ST - 1,
                                   pattern=[[0, 1]], channel_multiplier=-1)
            for fill, base in ((-1.0, -ST), (1.0, ST)):
                pool.affine_select(out=turn[:, :], in_=turn[:, :], compare_op=ALU.not_equal, fill=fill,
                                   base=base, pattern=[[-1, 128]], channel_multiplier=1).then_inc(s_ident, 1)
                pool.wait_ge(s_ident, 5 + (base > 0))
    return {"ident": ident, "eps": eps, "sgn": sgn, "nsgn": nsgn, "turn": turn}


def build(nc, t, stages=("proj", "ssm", "att", "satt", "mix", "ffn")):
    for name, shape in (("mod", [1 + NB, NMOD * D]), ("q", [ROWS, AW]), ("k_new", [NS, AW]), ("v_new", [NS, AW]),
                        ("u", [ROWS, SW]), ("y", [ROWS, SW]), ("zc", [BLKS, 128, Z_COLS]), ("o", [len(DILATIONS), SEQ, OROW]),
                        ("att_new", [NS, AW]), ("x1", [ROWS, D]), ("h2T", [128, KT, ROWS])):
        if name not in t:
            t[name] = nc.dram_tensor("scratch_" + name, shape, F32, kind="Internal").ap()
    with ExitStack() as ctx:
        P = Pool_(nc, ctx)
        const = constants(nc, P)
        const.update(o_stored=P.sem2("o_stored"), h2_stored=P.sem2("h2_stored"), windows_moved=P.sem("windows_moved"))
        with ExitStack() as c2:
            P2 = Pool_(nc, c2)
            w_in_sb = P2.sb("w_in_sb", [128, KT, 2 * D])
            s_win = P.sem("s_win")
            if "proj" in stages:
                modulation_stage(nc, t, const, w_in_sb, s_win)
                projection_stage(nc, t, const, w_in_sb, s_win)
        if "ssm" in stages:
            keep = {"pw": P.sb("keep_pw", [128, 2, GROUPS, LC + 1]), "rho8": P.sb("keep_rho8", [128, GROUPS]),
                    "e8": P.sb("keep_e8", [128, 2, GROUPS]), **const}
            state_space_constants_stage(nc, t, const, keep)
            state_space_stage(nc, t, const, keep)
        if "att" in stages:
            attention_stage(nc, t, const)
        if "satt" in stages:
            sample_attention_stage(nc, t, const)
        if "mix" in stages:
            mix_stage(nc, t, const)
        if "ffn" in stages:
            ffn_stage(nc, t, const)


INS = ('x_prompt', 'x_sample', 'cache_k', 'cache_v', 'state_ssm_re', 'state_ssm_im', 'c_prompt', 'c_sample',
       'norm1_g', 'norm2_g', 'w_ada', 'b_ada', 'w_in', 'q_gain', 'k_gain', 'ssm_a_re', 'ssm_a_im', 'ssm_log_dt',
       'ssm_b_re', 'ssm_b_im', 'ssm_c_re', 'ssm_c_im', 'ssm_d', 'w_glu', 'attn_out_g', 'ssm_out_g', 'w_out',
       'w_gate', 'w_up', 'w_down')
OUTS = (('y_prompt', (SEQ, D), (1, SEQ, D)), ('y_sample', (NS, D), (NB, TS, D)),
        ('k_prompt', (SEQ, AW), (1, 1, SEQ, HEADS, HD)), ('v_prompt', (SEQ, AW), (1, 1, SEQ, HEADS, HD)),
        ('ssm_re_prompt', (GROUPS, ST), (1, 1, GROUPS, ST)), ('ssm_im_prompt', (GROUPS, ST), (1, 1, GROUPS, ST)),
        ('k_sample', (NB, PAST, AW), (1, NB, PAST, HEADS, HD)), ('v_sample', (NB, PAST, AW), (1, NB, PAST, HEADS, HD)),
        ('ssm_re_sample', (NB, GROUPS, ST), (1, NB, GROUPS, ST)), ('ssm_im_sample', (NB, GROUPS, ST), (1, NB, GROUPS, ST)))
FLAT = {'x_prompt': (SEQ, D), 'x_sample': (NS, D), 'cache_k': (NB, PAST, AW), 'cache_v': (NB, PAST, AW),
        'c_prompt': (1, D), 'c_sample': (NB, D)}


def kernel(**inputs):
    import numpy as _np
    import concourse.bacc as _bacc
    from concourse import mybir as _mybir
    from concourse.bass_utils import run_bass_kernel_spmd as _run

    nc = _bacc.Bacc("TRN2", target_bir_lowering=False, num_devices=1)
    arrays, t = {}, {}
    for name in INS:
        a = _np.asarray(inputs[name])
        a = _np.ascontiguousarray(a.reshape(FLAT[name] if name in FLAT else a.shape[1:]))
        arrays[f"in_{name}_dram"] = a
        t[name] = nc.dram_tensor(f"in_{name}_dram", a.shape, _mybir.dt.from_np(a.dtype), kind="ExternalInput").ap()
    for i, (name, shape, _) in enumerate(OUTS):
        t[name] = nc.dram_tensor(f"out_{i}_dram", shape, F32, kind="ExternalOutput").ap()
    build(nc, t)
    r = _run(nc, [arrays], core_ids=[0])
    return tuple(r.results[0][f"out_{i}_dram"].reshape(shape) for i, (_, _, shape) in enumerate(OUTS))
```
